# Optimizing a Trainium2 kernel written in Bass

```python
import math
import jax, jax.numpy as jnp
from jax import lax
import numpy as np

D_MODEL = 1024
BATCH = 1
SEQ = 256
DEPTH = 2

MIX_A = 512
SGU_GROUPS = 4
SGU_DG = MIX_A // SGU_GROUPS
CHUNK = 128
N_Q_HEADS = 8
N_KV_HEADS = 2
HEAD_DIM = 64
GQ = N_Q_HEADS // N_KV_HEADS
MIX_B = N_Q_HEADS * HEAD_DIM
MIX_WIDTH = MIX_A + MIX_B
WINDOW = 128
BLOCK = 128
N_BUCKETS = 32
MAX_DISTANCE = 128
D_FF = 2816
IN_COLS = 2 * MIX_A + MIX_B + 2 * N_KV_HEADS * HEAD_DIM
EPS = 1e-6
NEG_INF = -1e30

kernel_name = "hybrid_sgu_swa_macaron_encoder"

def _rmsnorm(x, g):
    x32 = x.astype(jnp.float32)
    inv = lax.rsqrt(jnp.mean(x32 * x32, axis=-1, keepdims=True) + EPS)
    return (x32 * inv).astype(x.dtype) * g

def _swiglu(h, w_in, w_out):
    gu = h @ w_in
    gate, up = jnp.split(gu, 2, axis=-1)
    return (jax.nn.silu(gate) * up) @ w_out

def _t5_bucket(rel):
    nb = N_BUCKETS // 2
    ret = (rel > 0).astype(np.int32) * nb
    n = np.abs(rel)
    max_exact = nb // 2
    large = max_exact + (np.log(np.maximum(n, 1).astype(np.float32) / max_exact)
                         / math.log(MAX_DISTANCE / max_exact) * (nb - max_exact)).astype(np.int32)
    large = np.minimum(large, nb - 1)
    return ret + np.where(n < max_exact, n, large).astype(np.int32)

def _spatial_gating(a_proj, norm_g, w_s, b_s):
    B, S, _ = a_proj.shape
    z = jax.nn.gelu(a_proj)
    u, v = jnp.split(z, 2, axis=-1)
    v = _rmsnorm(v.reshape(B, S, SGU_GROUPS, SGU_DG), norm_g.reshape(SGU_GROUPS, SGU_DG))
    vc = v.reshape(B, S // CHUNK, CHUNK, SGU_GROUPS, SGU_DG)
    s = jnp.einsum('gpq,bcqgd->bcpgd', w_s, vc) + b_s.T[:, :, None]
    return u * s.reshape(B, S, MIX_A)

def _windowed_gqa(q, k, v, q_g, k_g, sink, rel_bias):
    B, S, _ = q.shape
    nB = S // BLOCK
    q = _rmsnorm(q.reshape(B, S, N_Q_HEADS, HEAD_DIM), q_g)
    k = _rmsnorm(k.reshape(B, S, N_KV_HEADS, HEAD_DIM), k_g)
    v = v.reshape(B, S, N_KV_HEADS, HEAD_DIM)
    pad = ((0, 0), (BLOCK, BLOCK), (0, 0), (0, 0))
    kp = jnp.pad(k, pad).reshape(B, nB + 2, BLOCK, N_KV_HEADS, HEAD_DIM)
    vp = jnp.pad(v, pad).reshape(B, nB + 2, BLOCK, N_KV_HEADS, HEAD_DIM)
    kw = jnp.concatenate([kp[:, :-2], kp[:, 1:-1], kp[:, 2:]], axis=2)
    vw = jnp.concatenate([vp[:, :-2], vp[:, 1:-1], vp[:, 2:]], axis=2)
    qb = q.reshape(B, nB, BLOCK, N_KV_HEADS, GQ, HEAD_DIM)
    s = jnp.einsum('bnqhgd,bnkhd->bnhgqk', qb, kw).astype(jnp.float32) * (HEAD_DIM ** -0.5)
    rel = np.arange(3 * BLOCK)[None, :] - BLOCK - np.arange(BLOCK)[:, None]
    bias = rel_bias[_t5_bucket(rel)]
    bias = jnp.transpose(bias, (2, 0, 1)).reshape(N_KV_HEADS, GQ, BLOCK, 3 * BLOCK).astype(jnp.float32)
    key_pos = np.arange(nB)[:, None] * BLOCK + np.arange(3 * BLOCK)[None, :] - BLOCK
    valid = (np.abs(rel) <= WINDOW)[None] & ((key_pos >= 0) & (key_pos < S))[:, None, :]
    s = jnp.where(jnp.asarray(valid)[None, :, None, None], s + bias, NEG_INF)
    sink_l = sink.astype(jnp.float32).reshape(N_KV_HEADS, GQ)[None, None, :, :, None, None]
    m = jnp.maximum(jnp.max(s, axis=-1, keepdims=True), sink_l)
    p = jnp.exp(s - m)
    p = p / (jnp.sum(p, axis=-1, keepdims=True) + jnp.exp(sink_l - m))
    o = jnp.einsum('bnhgqk,bnkhd->bnqhgd', p.astype(vw.dtype), vw)
    return o.reshape(B, S, MIX_B)

def setup_inputs(seed: int = 0) -> dict:
    key = jax.random.key(seed)
    ks = jax.random.split(key, 20)
    f = jnp.float32
    nrm = lambda k, shape, scale: jax.random.normal(k, shape, f) * scale
    gain = lambda k, shape: 1.0 + 0.05 * jax.random.normal(k, shape, f)
    return {
        "x": jax.random.normal(ks[0], (BATCH, SEQ, D_MODEL), f),
        "ffn1_norm": gain(ks[1], (DEPTH, D_MODEL)),
        "ffn1_w_in": nrm(ks[2], (DEPTH, D_MODEL, 2 * D_FF), D_MODEL ** -0.5),
        "ffn1_w_out": nrm(ks[3], (DEPTH, D_FF, D_MODEL), D_FF ** -0.5),
        "mix_norm": gain(ks[4], (DEPTH, D_MODEL)),
        "w_mix_in": nrm(ks[5], (DEPTH, D_MODEL, IN_COLS), D_MODEL ** -0.5),
        "sgu_norm": gain(ks[6], (DEPTH, MIX_A)),
        "sgu_w": nrm(ks[7], (DEPTH, SGU_GROUPS, CHUNK, CHUNK), 0.5 * CHUNK ** -0.5),
        "sgu_b": gain(ks[8], (DEPTH, SGU_GROUPS, CHUNK)),
        "q_norm": gain(ks[9], (DEPTH, HEAD_DIM)),
        "k_norm": gain(ks[10], (DEPTH, HEAD_DIM)),
        "sink": nrm(ks[11], (DEPTH, N_Q_HEADS), 0.5),
        "rel_bias": nrm(ks[12], (N_BUCKETS, N_Q_HEADS), 0.5),
        "w_mix_out": nrm(ks[13], (DEPTH, MIX_WIDTH, D_MODEL), MIX_WIDTH ** -0.5),
        "ffn2_norm": gain(ks[14], (DEPTH, D_MODEL)),
        "ffn2_w_in": nrm(ks[15], (DEPTH, D_MODEL, 2 * D_FF), D_MODEL ** -0.5),
        "ffn2_w_out": nrm(ks[16], (DEPTH, D_FF, D_MODEL), D_FF ** -0.5),
    }

def reference(x, ffn1_norm, ffn1_w_in, ffn1_w_out, mix_norm, w_mix_in, sgu_norm, sgu_w, sgu_b,
              q_norm, k_norm, sink, rel_bias, w_mix_out, ffn2_norm, ffn2_w_in, ffn2_w_out):
    for l in range(DEPTH):
        x = x + 0.5 * _swiglu(_rmsnorm(x, ffn1_norm[l]), ffn1_w_in[l], ffn1_w_out[l])
        h = _rmsnorm(x, mix_norm[l])
        p = h @ w_mix_in[l]
        a_proj = p[..., :2 * MIX_A]
        q = p[..., 2 * MIX_A:2 * MIX_A + MIX_B]
        kv_w = N_KV_HEADS * HEAD_DIM
        k = p[..., 2 * MIX_A + MIX_B:2 * MIX_A + MIX_B + kv_w]
        v = p[..., 2 * MIX_A + MIX_B + kv_w:]
        out_a = _spatial_gating(a_proj, sgu_norm[l], sgu_w[l], sgu_b[l])
        out_b = _windowed_gqa(q, k, v, q_norm[l], k_norm[l], sink[l], rel_bias)
        x = x + jnp.concatenate([out_a, out_b], axis=-1) @ w_mix_out[l]
        x = x + 0.5 * _swiglu(_rmsnorm(x, ffn2_norm[l]), ffn2_w_in[l], ffn2_w_out[l])
    return x


_drawn_inputs = setup_inputs


def setup_inputs(seed=0):
    import zlib

    import numpy as np

    out = dict(_drawn_inputs(seed))
    spreads = {}
    factors = {'sgu_norm': 3.929, 'q_norm': 8.0, 'k_norm': 8.0, 'sink': 8.0}
    for name, (base, spread) in spreads.items():
        noise = np.random.default_rng([zlib.crc32(name.encode()), seed]).standard_normal(out[name].shape)
        drawn = base * np.exp(spread * noise) if base else spread * noise
        out[name] = __import__('jax').numpy.asarray(drawn.astype(out[name].dtype))
    for name, factor in factors.items():
        out[name] = (out[name] * factor).astype(out[name].dtype)
    return out
```

```python
from contextlib import ExitStack

import numpy as np

import concourse.bass as bass
from concourse import mybir

F32 = mybir.dt.float32
F32R = mybir.dt.float32r
BF16 = mybir.dt.bfloat16
ACT = mybir.ActivationFunctionType
ALU = mybir.AluOpType
AX_X = mybir.AxisListType.X

P = 128
EPS = 1e-6
NEG_INF = -1e30
WINDOW = 128
N_BUCKETS = 32
MAX_DISTANCE = 128

SLOTS = 6
RAW = 3
UNIT = 2048
FC = 256

LAYER_POS = 78
EMPTY = 44
LAYER_UNITS = LAYER_POS - 1
FFN_BASE = (0, 45)
POS_KV, POS_Q, POS_V, POS_U, POS_OUT = 33, 34, 36, 38, 40
RAW_UNITS = tuple(len([p for p in range(LAYER_POS) if p % RAW == r and p != EMPTY]) for r in range(RAW))


def nth(p):
    return p if p < EMPTY else p - 1


def pos_in(f, c, u):
    return FFN_BASE[f] + (u if c == 0 else 3 * c - 1 + u)


def pos_out(f, c):
    return FFN_BASE[f] + (3 * c + 4 if c < 10 else 32)


def bucket_of(rel):
    nb = N_BUCKETS // 2
    n = np.abs(rel)
    exact = nb // 2
    large = exact + (np.log(np.maximum(n, 1).astype(np.float32) / exact)
                     / np.log(MAX_DISTANCE / exact) * (nb - exact)).astype(np.int32)
    return (rel > 0).astype(np.int32) * nb + np.where(n < exact, n, np.minimum(large, nb - 1))


def runs_of_buckets():
    rel = np.arange(-WINDOW, WINDOW + 1)
    b = bucket_of(rel)
    cuts = [0] + [i for i in range(1, len(b)) if b[i] != b[i - 1]] + [len(b)]
    return [(int(rel[a]), int(rel[z - 1]) + 1, int(b[a])) for a, z in zip(cuts, cuts[1:])]


FILLS = ["ws", "k0", "q0", "k1", "q1", "p0a", "p0b", "p1a", "p1b", "p2a", "p2b", "o0", "p3a", "p3b", "a0", "a1", "o1"]
BY_ACT = [n for n in FILLS if not n.endswith("b")]
BY_DVE = [n for n in FILLS if n.endswith("b") or n[0] in "oa"]
PROJ = ["KV", "Q", "V", "U"]
TAKEN = ["KV0", "Q0", "KV1", "Q1", "V0", "V1", "U0", "U1"]
NORMED = ["K0", "Q0", "K1", "Q1", "V0", "V1"]


def encoder(nc, x, ffn1_norm, ffn1_w_in, ffn1_w_out, mix_norm, w_mix_in, sgu_norm, sgu_w, sgu_b,
            q_norm, k_norm, sink, rel_bias, w_mix_out, ffn2_norm, ffn2_w_in, ffn2_w_out, out):
    _, S, D = x.shape
    DEPTH = ffn1_w_in.shape[0]
    DFF = ffn1_w_out.shape[1]
    NCH = DFF // FC
    MIX_A = sgu_norm.shape[1]
    NG = sgu_w.shape[1]
    HD = q_norm.shape[1]
    NH = sink.shape[1]
    KT = D // P
    assert S == 2 * P and NCH == 11 and D == 1024 and MIX_A == 512 and NH == 8 and HD == 64 and NG == 4

    w_in = [w.rearrange("l (k p) n -> l p k n", p=P) for w in (ffn1_w_in, ffn2_w_in)]
    w_out = [w.rearrange("l (k p) n -> l p k n", p=P) for w in (ffn1_w_out, ffn2_w_out)]
    mix_in = w_mix_in.rearrange("l (k p) n -> l p k n", p=P)
    mix_out = w_mix_out.rearrange("l (k p) n -> l p k n", p=P)
    x_tiles = x.rearrange("b (t p) d -> (b t) p d", p=P)
    out_tiles = out.rearrange("b (t p) d -> (b t) p d", p=P)
    RELS = 2 * S - 1
    bias_rows = nc.dram_tensor("bias_rows", (NH, P, RELS), F32, kind="Internal").ap()

    with ExitStack() as ctx:
        def sb(name, shape, dt=F32):
            return ctx.enter_context(nc.sbuf_tensor(name, shape, dt))

        def bank(name):
            return ctx.enter_context(nc.psum_tensor(name, [P, 512], F32))

        def sem(name):
            return ctx.enter_context(nc.semaphore(name))

        raw = sb("raw", [P, RAW, UNIT])
        w_hi = sb("w_hi", [P, SLOTS, UNIT], F32R)
        w_lo = sb("w_lo", [P, SLOTS, UNIT], F32R)
        xs = sb("xs", [P, 2, D])
        xT_hi = sb("xT_hi", [P, KT, S], F32R)
        xT_lo = sb("xT_lo", [P, KT, S], F32R)
        hT_hi = sb("hT_hi", [P, 2, 2, S], F32R)
        hT_lo = sb("hT_lo", [P, 2, 2, S], F32R)
        small = sb("small", [P, 4, FC])
        gate, h = small[:, 0:2, :], small[:, 2:4, :]
        pT = small[:, :, :].rearrange("p (a b) n -> p a (b n)", a=2)
        sc = sb("sc", [P, 2, 4, S])
        xg = sc[:, 0, :, :].rearrange("p (a b) n -> p a (b n)", a=2)
        bias = sb("bias", [P, NH, 3 * P])
        qs = sb("qs", [P, 2, MIX_A])
        kv = sb("kv", [P, 2, 4 * HD])
        kd = sb("kd", [P, 2, 2, P])
        qT = sb("qT", [P, 2, 4, P])
        kT = sb("kT", [P, 2, S])
        gv = sb("gv", [P, 2, MIX_A])
        wsT = sb("wsT", [P, NG * P])
        o = sb("o", [P, NH * HD])
        sq = sb("sq", [P, MIX_A])
        ws = sb("ws", [P, NG, P])
        sgain = sb("sgain", [P, MIX_A])
        sinks = sb("sinks", [P, NH])
        ident = sb("ident", [P, P])
        NROW = 60
        rows = wsT[0:NROW, 0:P]
        gall = sb("gall", [P, NROW])
        gcur = sb("gcur", [P, 3 * KT + 2 + NG])
        G_Q, G_K, G_B = 3 * KT, 3 * KT + 1, 3 * KT + 2
        ms = sb("ms", [P, 2])
        inv = sb("inv", [P, 2])
        mean = sb("mean", [P, 32])
        mhalf = sb("mhalf", [P, NH])
        sums = sb("sums", [P, 32])
        rstd = sb("rstd", [P, 32])
        mx = sb("mx", [P, 2 * NH])
        nmx = sb("nmx", [P, 2 * NH])
        sd = sb("sd", [P, 2 * NH])
        den = sb("den", [P, 2 * NH])
        esink = sb("esink", [P, 2 * NH])
        dtot = sb("dtot", [P, 2 * NH])
        rden = sb("rden", [P, 2 * NH])
        rb = sb("rb", [NH, N_BUCKETS])
        brow = o[0:NH, 0:RELS]

        U = [bank("U0"), bank("U1")]
        acc = [[bank("C0"), bank("C1")], [bank("D0"), bank("D1")]]
        C0, C1 = acc[0]
        TR = [bank("TR0"), bank("TR1")]
        PROJ_BANK = {"KV0": U[0], "KV1": U[1], "Q0": C0, "Q1": C1, "V0": U[0], "V1": U[1],
                     "U0": acc[1][0], "U1": acc[1][1]}

        x_loaded = [sem("x_loaded0"), sem("x_loaded1")]
        rows_loaded = sem("rows_loaded")
        rb_loaded = sem("rb_loaded")
        bias_stored = sem("bias_stored")
        bias_loaded = sem("bias_loaded")
        mix_params = sem("mix_params")
        consts_ready = sem("consts_ready")
        rows_T = sem("rows_T")
        gall_ready = sem("gall_ready")
        brow_ready = sem("brow_ready")
        unit_loaded = [sem(f"unit_loaded{r}") for r in range(RAW)]
        hi_ready = sem("hi_ready")
        lo_ready = sem("lo_ready")
        units_used = sem("units_used")
        gu_ready = sem("gu_ready")
        silu_done = sem("silu_done")
        h_done = sem("h_done")
        hT_psum = sem("hT_psum")
        hT_hi_done = sem("hT_hi_done")
        hT_lo_done = sem("hT_lo_done")
        acc_ready = sem("acc_ready")
        x_new = sem("x_new")
        xT_psum = sem("xT_psum")
        xg_done = sem("xg_done")
        xT_hi_done = sem("xT_hi_done")
        xT_lo_done = sem("xT_lo_done")
        ms_done = sem("ms_done")
        inv_done = sem("inv_done")
        proj_ready = sem("proj_ready")
        proj_taken = sem("proj_taken")
        sq_done = sem("sq_done")
        sums_done = sem("sums_done")
        rstd_done = sem("rstd_done")
        k_normed = sem("k_normed")
        q_normed = sem("q_normed")
        v_normed = sem("v_normed")
        tr_filled = sem("tr_filled")
        tr_act = sem("tr_act")
        tr_dve = sem("tr_dve")
        scores_ready = sem("scores_ready")
        scores_biased = sem("scores_biased")
        probs_ready = sem("probs_ready")
        pv_ready = sem("pv_ready")
        o_done = sem("o_done")
        sg_ready = sem("sg_ready")
        a_done = sem("a_done")
        pool_step = sem("pool_step")
        dve_step = sem("dve_step")
        stored = sem("stored")
        turns_sp, turns_pool, turns_dve = sem("turns_sp"), sem("turns_pool"), sem("turns_dve")

        def n_unit(L, p, j=0):
            return L * LAYER_UNITS + j * 6 + (nth(p) + 1)

        def n_used(L, p, j=0):
            return L * LAYER_UNITS + j * 6 + (SLOTS + nth(p) + 1)

        def n_slot_free(L, p, j=0):
            if p < SLOTS:
                return L * LAYER_UNITS + (p + 1)
            return n_used(L, p - SLOTS if p - SLOTS != EMPTY else p - 2 * SLOTS, j)

        def n_raw_free(L, p, j=0):
            if p < RAW:
                return L * LAYER_UNITS + (p + 1)
            q = p - RAW if p - RAW != EMPTY else p - 2 * RAW
            return L * LAYER_UNITS + j * 6 + (RAW + nth(q) + 1)

        def n_loaded(L, p, j=0):
            k = p // RAW - (1 if p > EMPTY and p % RAW == EMPTY % RAW else 0)
            return L * (32 * RAW_UNITS[p % RAW]) + j * 64 + 32 * (k + 1)

        def n_ffn(L, f, c, t, j=0):
            return L * (4 * NCH) + j * 4 + (2 * NCH * f + 2 * c + t + 1)

        def n_gu(L, f, c, j=0):
            return L * (2 * NCH) + j * 2 + (NCH * f + c + 1)

        def n_tran(L, q, t, half):
            return L * 12 + (4 * q + 2 * t + half + 1)

        def n_x_new(L, ph, t, half):
            return L * 12 + (4 * (ph + 1) + 2 * t + half + 1)

        def n_inv(L, q, t):
            return L * 6 + (2 * q + t + 1)

        def n_of(L, names, name):
            return L * len(names) + (names.index(name) + 1)

        block = ctx.enter_context(nc.Block())

        @block.sync
        def _(sp):
            def load(L, p, parts, j=0):
                sp.wait_ge(lo_ready, n_raw_free(L, p, j))
                sp.sem_inc(turns_sp, 1)
                dst = raw[:, p % RAW, :]
                for d, s in parts(dst):
                    sp.dma_start(d, s).then_inc(unit_loaded[p % RAW], 16)

            def load_in(L, f, c, u, j=0):
                def parts(dst):
                    d = dst.rearrange("p (k g n) -> p k g n", k=4, g=2)
                    for g in range(2):
                        cols = bass.ds(j * (2 * FC) + (g * DFF + c * FC), FC)
                        yield d[:, :, g, :], w_in[f][bass.ds(L, 1), :, 4 * u:4 * u + 4, cols][0]
                load(L, pos_in(f, c, u), parts, j)

            def load_out(L, f, c, j=0):
                def parts(dst):
                    for kk in range(2):
                        yield (dst[:, kk * D:(kk + 1) * D],
                               w_out[f][bass.ds(L, 1), :, bass.ds(j * 4 + (2 * c + kk), 1), :][0, :, 0, :])
                load(L, pos_out(f, c), parts, j)

            def load_mix(L, p, col, width, k0):
                def parts(dst):
                    n = UNIT // width // 2
                    d = dst.rearrange("p (k n) -> p k n", n=width)
                    for i in range(2):
                        yield (d[:, i * n:(i + 1) * n, :],
                               mix_in[bass.ds(L, 1), :, k0 + i * n:k0 + (i + 1) * n, col:col + width][0])
                load(L, p, parts)

            def load_mix_out(L, i):
                def parts(dst):
                    for kk in range(2):
                        yield dst[:, kk * D:(kk + 1) * D], mix_out[bass.ds(L, 1), :, 2 * i + kk, :][0]
                load(L, POS_OUT + i, parts)

            def ffn_weights(L, f):
                load_in(L, f, 0, 0)
                load_in(L, f, 0, 1)

                def chunk(c, j=0):
                    load_in(L, f, c + 1, 0, j)
                    load_in(L, f, c + 1, 1, j)
                    load_out(L, f, c, j)
                chunk(0)
                with sp.Fori(0, 4) as j:
                    chunk(1, j)
                    chunk(2, j)
                chunk(9)
                load_out(L, f, 10)

            for t in range(2):
                sp.dma_start(xs[:, t, :], x_tiles[t]).then_inc(x_loaded[t], 16)
            with sp.Fori(0, DEPTH) as L:
                ffn_weights(L, 0)
                load_mix(L, POS_KV, 3 * MIX_A, 4 * HD, 0)
                for i, (p, col) in enumerate([(POS_Q, 2 * MIX_A), (POS_V, MIX_A), (POS_U, 0)]):
                    for u in range(2):
                        load_mix(L, p + u, col, MIX_A, 4 * u)
                for i in range(4):
                    load_mix_out(L, i)
                ffn_weights(L, 1)
            for t in range(2):
                sp.wait_ge(x_new, n_x_new(DEPTH - 1, 2, t, 1))
                sp.dma_start(out_tiles[t], xs[:, t, :]).then_inc(stored, 16)
            sp.wait_ge(stored, 32)

        @block.gpsimd
        def _(pool):
            steps = 0

            def step(ins, L=0, count=True):
                nonlocal steps
                steps += 1
                ins.then_inc(pool_step, 1)
                pool.wait_ge(pool_step, L * per_layer + steps)

            per_layer = 0
            for r0, v in ((0, ffn1_norm), (16, mix_norm), (32, ffn2_norm)):
                pool.dma_start(rows[r0:r0 + 2 * KT, :], v.rearrange("l (k p) -> (l k) p", p=P)).then_inc(rows_loaded, 16)
            for r0, v in ((48, q_norm), (50, k_norm)):
                for i in range(2):
                    pool.dma_start(rows[r0:r0 + 2, i * HD:(i + 1) * HD], v).then_inc(rows_loaded, 16)
            pool.dma_start(rows[52:60, :], sgu_b.rearrange("l g p -> (l g) p")).then_inc(rows_loaded, 16)
            step(pool.memset(ident[:, :], 0.0))
            step(pool.affine_select(out=ident[:, :], in_=ident[:, :], compare_op=ALU.not_equal, fill=1.0,
                                    base=0, pattern=[[-1, P]], channel_multiplier=1))
            pool.memset(mhalf[:, :], -0.5).then_inc(consts_ready, 1)
            with nc.allow_non_contiguous_dma(reason="256 numbers, once"):
                pool.dma_start(rb[:, :], rel_bias.rearrange("b h -> h b")).then_inc(rb_loaded, 16)
            pool.wait_ge(brow_ready, 1)
            pool.dma_start(bias_rows, brow.unsqueeze(1).to_broadcast([NH, P, RELS])).then_inc(bias_stored, 16)
            pool.wait_ge(bias_stored, 16)
            for hh in range(NH):
                src = bass.AP(bias_rows.tensor, hh * P * RELS + (P - 1), [[RELS - 1, P], [1, 3 * P]])
                pool.dma_start(bias[:, hh, :], src).then_inc(bias_loaded, 16)

            def rsqrt(L, dst, src, tmp, n, width):
                pool.sem_inc(turns_pool, 1)
                step(pool.tensor_scalar(tmp, src, 1.0 / n, EPS, ALU.mult, ALU.add), L)
                return pool.tensor_tensor(dst, tmp, mhalf[:, 0:width], ALU.pow)

            def inverse_rms(L, q, t):
                pool.wait_ge(ms_done, n_inv(L, q, t))
                rsqrt(L, inv[:, t:t + 1], ms[:, t:t + 1], mean[:, 30 + t:31 + t], D, 1).then_inc(inv_done, 1)

            def squares(L, name, src, n):
                if name != "K0":
                    pool.wait_ge(sums_done, n_of(L, NORMED, NORMED[NORMED.index(name) - 1]))
                pool.wait_ge(proj_taken, n_of(L, TAKEN, name.replace("K", "KV")))
                pool.tensor_tensor(sq[:, 0:n], src, src, ALU.mult).then_inc(sq_done, 1)

            def norm(L, name, c0, groups, n):
                pool.wait_ge(sums_done, n_of(L, NORMED, name))
                return rsqrt(L, rstd[:, c0:c0 + groups], sums[:, c0:c0 + groups], mean[:, c0:c0 + groups], n, groups)

            base = steps
            inverse_rms(0, 0, 0)
            inverse_rms(0, 0, 1)
            per_layer = 6 + 2 + 4 + 6
            first = steps
            with pool.Fori(0, DEPTH) as L:
                pool.wait_ge(units_used, L * LAYER_UNITS + SLOTS)
                pool.dma_start(ws[:, :, :], sgu_w.rearrange("l g p q -> l p g q")[bass.ds(L, 1)][0]).then_inc(mix_params, 16)
                pool.dma_start(sgain[:, :], sgu_norm[bass.ds(L, 1), :].partition_broadcast(P)[:, 0, :]).then_inc(mix_params, 16)
                pool.dma_start(sinks[:, :], sink[bass.ds(L, 1), :].partition_broadcast(P)[:, 0, :]).then_inc(mix_params, 16)
                inverse_rms(L, 1, 0)
                inverse_rms(L, 1, 1)
                for t in range(2):
                    squares(L, f"K{t}", kv[:, t, 0:2 * HD], 2 * HD)
                    norm(L, f"K{t}", 2 * t, 2, HD).then_inc(rstd_done, 1)
                    squares(L, f"Q{t}", qs[:, t, :], MIX_A)
                    step(norm(L, f"Q{t}", 4 + 8 * t, NH, HD), L)
                    qv = qs[:, t, :].rearrange("p (h d) -> p h d", h=NH)
                    pool.tensor_tensor(qv, qv, rstd[:, 4 + 8 * t:12 + 8 * t].unsqueeze(2).to_broadcast([P, NH, HD]),
                                       ALU.mult).then_inc(q_normed, 1)
                pool.wait_ge(mix_params, L * 48 + 48)
                for t in range(2):
                    squares(L, f"V{t}", gv[:, t, :], MIX_A)
                    step(norm(L, f"V{t}", 20 + 4 * t, NG, P), L)
                    vv = gv[:, t, :].rearrange("p (g d) -> p g d", g=NG)
                    step(pool.tensor_tensor(vv, vv, rstd[:, 20 + 4 * t:24 + 4 * t].unsqueeze(2).to_broadcast([P, NG, P]),
                                            ALU.mult), L)
                    pool.tensor_tensor(gv[:, t, :], gv[:, t, :], sgain[:, :], ALU.mult).then_inc(v_normed, 1)
                for q in (2, 3):
                    inverse_rms(L, q, 0)
                    inverse_rms(L, q, 1)
                assert steps - first == per_layer, steps - first

        @block.scalar
        def _(act):
            def split(L, p, j=0):
                act.wait_ge(unit_loaded[p % RAW], n_loaded(L, p, j))
                act.wait_ge(units_used, n_slot_free(L, p, j))
                act.activation(w_hi[:, p % SLOTS, :], raw[:, p % RAW, :], ACT.Copy).then_inc(hi_ready, 1)

            def silu(L, f, c, t, j=0):
                if t == 0:
                    act.wait_ge(gu_ready, n_gu(L, f, c, j))
                else:
                    act.wait_ge(units_used, n_used(L, pos_in(f, c, 1), j))
                if c == 0:
                    act.wait_ge(inv_done, n_inv(L, 2 * f, t))
                else:
                    act.wait_ge(h_done, n_ffn(L, f, c - 1, t, j))
                act.activation(gate[:, t, :], U[t][:, 0:FC], ACT.Silu, scale=inv[:, t:t + 1]).then_inc(silu_done, 1)

            def take_hT(L, f, c, t, j=0):
                act.wait_ge(hT_psum, n_ffn(L, f, c, t, j))
                act.activation(hT_hi[:, c % 2, :, t * P:(t + 1) * P],
                               TR[t][:, 0:FC].rearrange("p (k n) -> p k n", k=2), ACT.Copy).then_inc(hT_hi_done, 1)

            def sum_squares(L, ph, t):
                if ph < 0:
                    act.wait_ge(x_loaded[t], 16)
                else:
                    act.wait_ge(x_new, n_x_new(L, ph, t, 1))
                if ph >= 0 or t == 1:
                    act.wait_ge(ms_done, n_inv(L, ph + 1, t) - 1)
                act.activation(sq[:, :].bitcast(BF16), xs[:, t, :], ACT.Square, accum_out=ms[:, t:t + 1]).then_inc(ms_done, 1)

            def take_xT(L, q, t):
                for half in range(2):
                    act.wait_ge(xg_done, n_tran(L, q, t, half))
                    act.activation(xT_hi[:, 4 * half:4 * half + 4, t * P:(t + 1) * P],
                                   xg[:, half, :].rearrange("p (k n) -> p k n", k=4), ACT.Copy).then_inc(xT_hi_done, 1)

            def ffn(L, f, after):
                def chunk(c, j=0):
                    if c > 0:
                        silu(L, f, c - 1, 1, j)
                    split(L, pos_in(f, c + 1, 0), j)
                    split(L, pos_in(f, c + 1, 1), j)
                    if c > 0:
                        take_hT(L, f, c - 1, 0, j)
                        take_hT(L, f, c - 1, 1, j)
                    silu(L, f, c, 0, j)
                    split(L, pos_out(f, c), j)
                chunk(0)
                with act.Fori(0, 4) as j:
                    chunk(1, j)
                    chunk(2, j)
                chunk(9)
                silu(L, f, 9, 1)
                split(L, pos_out(f, 10))
                take_hT(L, f, 9, 0)
                take_hT(L, f, 9, 1)
                silu(L, f, 10, 0)
                for p in after[0:2]:
                    split(L, p)
                silu(L, f, 10, 1)
                take_hT(L, f, 10, 0)
                for p in after[2:3]:
                    split(L, p)
                take_hT(L, f, 10, 1)
                sum_squares(L, 2 * f, 0)
                take_xT(L, 2 * f + 1, 0)
                for p in after[3:]:
                    split(L, p)
                sum_squares(L, 2 * f, 1)

            def take(L, name, dst, func, width):
                t = int(name[-1])
                if t == 0:
                    act.wait_ge(proj_ready, n_of(L, PROJ, name[:-1]))
                else:
                    last = {"KV": POS_KV, "Q": POS_Q + 1, "V": POS_V + 1, "U": POS_U + 1}[name[:-1]]
                    act.wait_ge(units_used, n_used(L, last))
                if name[:-1] == "KV":
                    act.wait_ge(inv_done, n_inv(L, 1, t))
                act.activation(dst, PROJ_BANK[name][:, 0:width], func, scale=inv[:, t:t + 1]).then_inc(proj_taken, 1)

            def evacuate(L, name, dst, width=512, scale=1.0):
                n = FILLS.index(name)
                act.wait_ge(tr_filled, n_of(L, FILLS, name))
                src = TR[n % 2][:, 0:width]
                if len(dst.shape) == 3:
                    src = src.rearrange("p (k n) -> p k n", k=dst.shape[1])
                act.activation(dst, src, ACT.Copy, scale=scale).then_inc(tr_act, 1)

            def exps(L, r):
                t, half = divmod(r, 2)
                act.wait_ge(scores_biased, L * 4 + (r + 1))
                for i in range(4):
                    c = t * NH + 4 * half + i
                    act.activation(sc[:, r % 2, i, :], sc[:, r % 2, i, :], ACT.Exp, bias=nmx[:, c:c + 1],
                                   accum_out=den[:, c:c + 1])
                c = t * NH + 4 * half
                act.activation(esink[:, c:c + 4], sd[:, c:c + 4], ACT.Exp).then_inc(probs_ready, 1)

            for t in range(2):
                sum_squares(0, -1, t)
            take_xT(0, 0, 0)
            with act.Fori(0, DEPTH) as L:
                split(L, 0)
                take_xT(L, 0, 1)
                split(L, 1)
                ffn(L, 0, [POS_KV, POS_Q, POS_Q + 1, POS_V])
                take_xT(L, 1, 1)
                take(L, "KV0", kv[:, 0, :], ACT.Copy, 4 * HD)
                split(L, POS_V + 1)
                take(L, "Q0", qs[:, 0, :], ACT.Copy, MIX_A)
                evacuate(L, "ws", wsT[:, :])
                split(L, POS_U)
                take(L, "KV1", kv[:, 1, :], ACT.Copy, 4 * HD)
                split(L, POS_U + 1)
                evacuate(L, "k0", kT[:, :, 0:P], 2 * P, gcur[:, G_K:G_K + 1])
                evacuate(L, "q0", qT[:, 0, :, :], 512, gcur[:, G_Q:G_Q + 1])
                take(L, "Q1", qs[:, 1, :], ACT.Copy, MIX_A)
                evacuate(L, "k1", kT[:, :, P:2 * P], 2 * P, gcur[:, G_K:G_K + 1])
                split(L, POS_OUT)
                evacuate(L, "q1", qT[:, 1, :, :], 512, gcur[:, G_Q:G_Q + 1])
                exps(L, 0)
                split(L, POS_OUT + 1)
                exps(L, 1)
                take(L, "V0", gv[:, 0, :], ACT.Gelu_apprx_tanh, MIX_A)
                evacuate(L, "p0a", pT[:, 0, :])
                take(L, "V1", gv[:, 1, :], ACT.Gelu_apprx_tanh, MIX_A)
                exps(L, 2)
                evacuate(L, "p1a", pT[:, 0, :])
                split(L, POS_OUT + 2)
                exps(L, 3)
                take(L, "U0", qs[:, 0, :], ACT.Gelu_apprx_tanh, MIX_A)
                evacuate(L, "p2a", pT[:, 0, :])
                evacuate(L, "o0", xT_hi[:, 4:8, 0:P])
                split(L, POS_OUT + 3)
                take(L, "U1", qs[:, 1, :], ACT.Gelu_apprx_tanh, MIX_A)
                evacuate(L, "p3a", pT[:, 0, :])
                evacuate(L, "a0", xT_hi[:, 0:4, 0:P])
                evacuate(L, "a1", xT_hi[:, 0:4, P:2 * P])
                split(L, FFN_BASE[1])
                evacuate(L, "o1", xT_hi[:, 4:8, P:2 * P])
                split(L, FFN_BASE[1] + 1)
                sum_squares(L, 1, 0)
                take_xT(L, 2, 0)
                sum_squares(L, 1, 1)
                take_xT(L, 2, 1)
                ffn(L, 1, [])

        @block.vector
        def _(dve):
            steps = 0
            per_layer = 0

            def step(ins, L=0):
                nonlocal steps
                steps += 1
                ins.then_inc(dve_step, 1)
                dve.wait_ge(dve_step, L * per_layer + steps)

            def split(L, p, j=0):
                dve.wait_ge(hi_ready, n_unit(L, p, j))
                dve.tensor_tensor(w_lo[:, p % SLOTS, :], raw[:, p % RAW, :], w_hi[:, p % SLOTS, :].bitcast(F32),
                                  ALU.subtract).then_inc(lo_ready, 1)

            def mul(L, f, c, t, j=0):
                dve.wait_ge(silu_done, n_ffn(L, f, c, t, j))
                dve.scalar_tensor_tensor(out=h[:, t, :], in0=U[t][:, FC:2 * FC], scalar=inv[:, t:t + 1],
                                         in1=gate[:, t, :], op0=ALU.mult, op1=ALU.mult).then_inc(h_done, 1)

            def take_hT(L, f, c, t, j=0):
                dve.wait_ge(hT_hi_done, n_ffn(L, f, c, t, j))
                cols = slice(t * P, (t + 1) * P)
                dve.tensor_tensor(hT_lo[:, c % 2, :, cols], TR[t][:, 0:FC].rearrange("p (k n) -> p k n", k=2),
                                  hT_hi[:, c % 2, :, cols].bitcast(F32), ALU.subtract).then_inc(hT_lo_done, 1)

            def residual(L, ph, t):
                if t == 0:
                    dve.wait_ge(acc_ready, L * 3 + (ph + 1))
                else:
                    dve.wait_ge(units_used, n_used(L, POS_OUT + 3 if ph == 1 else pos_out(ph // 2, 10)))
                for half in range(2):
                    xh = xs[:, t, half * 512:(half + 1) * 512]
                    dve.scalar_tensor_tensor(out=xh, in0=acc[t][half][:, :], scalar=1.0 if ph == 1 else 0.5, in1=xh,
                                             op0=ALU.mult, op1=ALU.add).then_inc(x_new, 1)

            def take_xT(L, q, t):
                g0 = {0: 2 * KT, 1: 0, 2: KT, 3: 2 * KT}[q]
                for half in range(2):
                    dve.wait_ge(xT_psum, n_tran(L, q, t, half))
                    gain = gcur[:, g0 + 4 * half:g0 + 4 * half + 4].unsqueeze(2).to_broadcast([P, 4, P])
                    dve.tensor_tensor(xg[:, half, :].rearrange("p (k n) -> p k n", k=4),
                                      TR[half][:, :].rearrange("p (k n) -> p k n", k=4), gain, ALU.mult).then_inc(xg_done, 1)
                for half in range(2):
                    dve.wait_ge(xT_hi_done, n_tran(L, q, t, half))
                    ks, cols = slice(4 * half, 4 * half + 4), slice(t * P, (t + 1) * P)
                    dve.tensor_tensor(xT_lo[:, ks, cols], xg[:, half, :].rearrange("p (k n) -> p k n", k=4),
                                      xT_hi[:, ks, cols].bitcast(F32), ALU.subtract).then_inc(xT_lo_done, 1)

            def ffn(L, f, after):
                def chunk(c, j=0):
                    if c > 0:
                        mul(L, f, c - 1, 1, j)
                    split(L, pos_in(f, c + 1, 0), j)
                    split(L, pos_in(f, c + 1, 1), j)
                    if c > 0:
                        take_hT(L, f, c - 1, 0, j)
                        take_hT(L, f, c - 1, 1, j)
                    if c == 0:
                        dve.wait_ge(inv_done, n_inv(L, 2 * f, 1))
                    mul(L, f, c, 0, j)
                    split(L, pos_out(f, c), j)
                chunk(0)
                with dve.Fori(0, 4) as j:
                    chunk(1, j)
                    chunk(2, j)
                chunk(9)
                mul(L, f, 9, 1)
                split(L, pos_out(f, 10))
                take_hT(L, f, 9, 0)
                take_hT(L, f, 9, 1)
                mul(L, f, 10, 0)
                for p in after[0:2]:
                    split(L, p)
                mul(L, f, 10, 1)
                take_hT(L, f, 10, 0)
                for p in after[2:3]:
                    split(L, p)
                take_hT(L, f, 10, 1)
                residual(L, 2 * f, 0)
                take_xT(L, 2 * f + 1, 0)
                for p in after[3:]:
                    split(L, p)
                residual(L, 2 * f, 1)

            def sum_of(L, name, c0, groups, n):
                dve.wait_ge(sq_done, n_of(L, NORMED, name))
                dve.tensor_reduce(sums[:, c0:c0 + groups], sq[:, 0:groups * n].rearrange("p (g n) -> p g n", g=groups),
                                  AX_X, ALU.add).then_inc(sums_done, 1)

            def scale_k(L, t):
                dve.wait_ge(rstd_done, L * 2 + (t + 1))
                for g in range(2):
                    last = dve.tensor_scalar(kd[:, t, g, :].rearrange("p (a d) -> p a d", a=2),
                                             kv[:, t, g * HD:(g + 1) * HD].unsqueeze(1).to_broadcast([P, 2, HD]),
                                             rstd[:, 2 * t + g:2 * t + g + 1], None, ALU.mult)
                last.then_inc(k_normed, 1)

            def biased(L, r):
                t, half = divmod(r, 2)
                dve.wait_ge(scores_ready, L * 4 + (r + 1))
                dve.sem_inc(turns_dve, 1)
                for i in range(4):
                    hh = 4 * half + i
                    c = t * NH + hh
                    ins = dve.tensor_tensor_reduce(
                        sc[:, r % 2, i, :], acc[0][i % 2][:, (i // 2) * S:(i // 2 + 1) * S],
                        bias[:, hh, (1 - t) * P:(1 - t) * P + S], 1.0, sinks[:, hh:hh + 1],
                        ALU.add, ALU.max, mx[:, c:c + 1])
                step(ins, L)
                c = t * NH + 4 * half
                dve.tensor_scalar(nmx[:, c:c + 4], mx[:, c:c + 4], -1.0, None, ALU.mult)
                dve.tensor_tensor(sd[:, c:c + 4], sinks[:, 4 * half:4 * half + 4], mx[:, c:c + 4],
                                  ALU.subtract).then_inc(scores_biased, 1)

            def evacuate(L, name, dst, src_hi=None):
                n = FILLS.index(name)
                if src_hi is None:
                    dve.wait_ge(tr_filled, n_of(L, FILLS, name))
                    dve.tensor_copy(dst, TR[n % 2][:, :]).then_inc(tr_dve, 1)
                else:
                    dve.wait_ge(tr_act, n_of(L, BY_ACT, name))
                    dve.tensor_tensor(dst, TR[n % 2][:, :].rearrange("p (k n) -> p k n", k=4), src_hi.bitcast(F32),
                                      ALU.subtract).then_inc(tr_dve, 1)

            def attended(L, t):
                cs = slice(t * NH, (t + 1) * NH)
                dve.wait_ge(probs_ready, L * 4 + (2 * t + 2))
                step(dve.tensor_tensor(dtot[:, cs], den[:, cs], esink[:, cs], ALU.add), L)
                step(dve.reciprocal(rden[:, cs], dtot[:, cs]), L)
                dve.wait_ge(pv_ready, L * 4 + (2 * t + 2))
                dve.tensor_tensor(o[:, :].rearrange("p (h d) -> p h d", h=NH),
                                  U[0][:, :].rearrange("p (h d) -> p h d", h=NH),
                                  rden[:, cs].unsqueeze(2).to_broadcast([P, NH, HD]), ALU.mult).then_inc(o_done, 1)

            def gated(L, t):
                dve.wait_ge(sg_ready, L * 2 + (t + 1))
                dve.wait_ge(proj_taken, n_of(L, TAKEN, f"U{t}"))
                for g in range(NG):
                    cols = slice(g * P, (g + 1) * P)
                    last = dve.scalar_tensor_tensor(out=qs[:, t, cols], in0=U[1][:, cols], scalar=gcur[:, G_B + g:G_B + g + 1],
                                                    in1=qs[:, t, cols], op0=ALU.add, op1=ALU.mult)
                last.then_inc(a_done, 1)

            dve.memset(brow, NEG_INF).then_inc(lo_ready, RAW)
            dve.memset(mx[:, :], 0.0).then_inc(units_used, SLOTS)
            for t in range(2):
                dve.wait_ge(x_loaded[t], 16)
            dve.sem_inc(x_new, 4)
            dve.wait_ge(rows_T, 1)
            dve.tensor_copy(gall[:, :], TR[0][:, 0:NROW]).then_inc(gall_ready, 1)
            dve.wait_ge(gall_ready, 1)
            step(dve.tensor_copy(gcur[:, 2 * KT:3 * KT], gall[:, 0:KT]))
            take_xT(0, 0, 0)
            dve.wait_ge(rb_loaded, 16)
            zero = WINDOW + P - 1
            for a, z, b in runs_of_buckets():
                last = dve.tensor_copy(brow[:, zero + a:zero + z], rb[:, b:b + 1].to_broadcast([NH, z - a]))
            last.then_inc(brow_ready, 1)

            first = steps
            per_layer = 6 + 4 + 4
            with dve.Fori(0, DEPTH) as L:
                split(L, 0)
                take_xT(L, 0, 1)
                split(L, 1)
                step(dve.tensor_copy(gcur[:, 0:KT], gall[:, bass.ds(L * KT + 2 * KT, KT)]), L)
                step(dve.tensor_copy(gcur[:, KT:2 * KT], gall[:, bass.ds(L * KT + 4 * KT, KT)]), L)
                step(dve.tensor_copy(gcur[:, 2 * KT:3 * KT], gall[:, bass.ds(L * KT + KT, KT)]), L)
                step(dve.tensor_scalar(gcur[:, G_Q:G_Q + 1], gall[:, bass.ds(L + 48, 1)], float(HD) ** -0.5, None, ALU.mult), L)
                step(dve.tensor_copy(gcur[:, G_K:G_K + 1], gall[:, bass.ds(L + 50, 1)]), L)
                step(dve.tensor_copy(gcur[:, G_B:G_B + NG], gall[:, bass.ds(L * NG + 52, NG)]), L)
                ffn(L, 0, [POS_KV, POS_Q, POS_Q + 1, POS_V])
                take_xT(L, 1, 1)
                sum_of(L, "K0", 0, 2, HD)
                split(L, POS_V + 1)
                scale_k(L, 0)
                sum_of(L, "Q0", 4, NH, HD)
                split(L, POS_U)
                sum_of(L, "K1", 2, 2, HD)
                split(L, POS_U + 1)
                scale_k(L, 1)
                sum_of(L, "Q1", 12, NH, HD)
                split(L, POS_OUT)
                dve.wait_ge(mix_params, L * 48 + 48)
                dve.wait_ge(bias_loaded, 16 * NH)
                biased(L, 0)
                split(L, POS_OUT + 1)
                biased(L, 1)
                sum_of(L, "V0", 20, NG, P)
                evacuate(L, "p0b", pT[:, 1, :])
                biased(L, 2)
                sum_of(L, "V1", 24, NG, P)
                evacuate(L, "p1b", pT[:, 1, :])
                split(L, POS_OUT + 2)
                attended(L, 0)
                biased(L, 3)
                gated(L, 0)
                evacuate(L, "p2b", pT[:, 1, :])
                evacuate(L, "o0", xT_lo[:, 4:8, 0:P], xT_hi[:, 4:8, 0:P])
                split(L, POS_OUT + 3)
                gated(L, 1)
                evacuate(L, "p3b", pT[:, 1, :])
                evacuate(L, "a0", xT_lo[:, 0:4, 0:P], xT_hi[:, 0:4, 0:P])
                attended(L, 1)
                evacuate(L, "a1", xT_lo[:, 0:4, P:2 * P], xT_hi[:, 0:4, P:2 * P])
                split(L, FFN_BASE[1])
                evacuate(L, "o1", xT_lo[:, 4:8, P:2 * P], xT_hi[:, 4:8, P:2 * P])
                split(L, FFN_BASE[1] + 1)
                residual(L, 1, 0)
                take_xT(L, 2, 0)
                residual(L, 1, 1)
                take_xT(L, 2, 1)
                ffn(L, 1, [])
                assert steps - first == per_layer, steps - first

        @block.tensor
        def _(pe):
            def split_ready(L, p, j=0):
                pe.wait_ge(lo_ready, L * LAYER_UNITS + j * 6 + (RAW + nth(p) + 1))

            def products(outs, x_hi, x_lo, slot, cols, start, stop):
                for out_, c in zip(outs, cols):
                    pe.matmul(out_, x_hi, w_hi[:, slot, c], start=start, stop=False)
                    pe.matmul(out_, x_hi, w_lo[:, slot, c], start=False, stop=False)
                for out_, c in zip(outs, cols):
                    last = pe.matmul(out_, x_lo, w_hi[:, slot, c], start=False, stop=stop)
                return last

            def project(L, p, t, u, dst, width, j=0):
                split_ready(L, p, j)
                n = UNIT // width
                for kk in range(n):
                    k = n * u + kk
                    last = products([dst], xT_hi[:, k, t * P:(t + 1) * P], xT_lo[:, k, t * P:(t + 1) * P], p % SLOTS,
                                    [slice(kk * width, (kk + 1) * width)], k == 0, k == KT - 1)
                if t == 1:
                    last.then_inc(units_used, 1)
                return last

            def sum_out(L, p, t, lhs_hi, lhs_lo, start, stop, j=0):
                split_ready(L, p, j)
                for kk in range(2):
                    last = products([acc[t][0][:, :], acc[t][1][:, :]], lhs_hi(kk), lhs_lo(kk), p % SLOTS,
                                    [slice(kk * D + n * 512, kk * D + (n + 1) * 512) for n in range(2)],
                                    start and kk == 0, stop and kk == 1)
                if t == 1:
                    last.then_inc(units_used, 1)
                return last

            def transpose_x(L, q, t):
                for half in range(2):
                    for i in range(4):
                        k = 4 * half + i
                        last = pe.transpose(TR[half][:, i * P:(i + 1) * P], xs[:, t, k * P:(k + 1) * P], ident[:, :])
                    last.then_inc(xT_psum, 1)

            def ffn(L, f):
                def enter(c, t, u, j=0):
                    if c == 0 and u == 0:
                        pe.wait_ge(xT_lo_done, n_tran(L, 2 * f, t, 1))
                    if c > 0 and u == 0:
                        pe.wait_ge(h_done, n_ffn(L, f, c - 1, t, j))
                    last = project(L, pos_in(f, c, u), t, u, U[t][:, :], 2 * FC, j)
                    if t == 0 and u == 1:
                        last.then_inc(gu_ready, 1)

                def transpose_h(c, t, j=0):
                    pe.wait_ge(h_done, n_ffn(L, f, c, t, j))
                    for kk in range(2):
                        last = pe.transpose(TR[t][:, kk * P:(kk + 1) * P], h[:, t, kk * P:(kk + 1) * P], ident[:, :])
                    last.then_inc(hT_psum, 1)

                def leave(c, t, j=0):
                    pe.wait_ge(hT_lo_done, n_ffn(L, f, c, t, j))
                    cols = slice(t * P, (t + 1) * P)
                    last = sum_out(L, pos_out(f, c), t, lambda kk: hT_hi[:, c % 2, kk, cols],
                                   lambda kk: hT_lo[:, c % 2, kk, cols], c == 0, c == NCH - 1, j)
                    if t == 0 and c == NCH - 1:
                        last.then_inc(acc_ready, 1)

                enter(0, 0, 0)
                if f == 1:
                    pe.wait_ge(x_new, n_x_new(L, 1, 1, 1))
                else:
                    pe.wait_ge(x_new, n_x_new(L, -1, 1, 1))
                pe.wait_ge(xg_done, n_tran(L, 2 * f, 0, 1))
                transpose_x(L, 2 * f, 1)
                enter(0, 0, 1)
                enter(0, 1, 0)
                enter(0, 1, 1)

                def chunk(c, j=0):
                    enter(c, 0, 0, j)
                    enter(c, 0, 1, j)
                    transpose_h(c - 1, 0, j)
                    transpose_h(c - 1, 1, j)
                    enter(c, 1, 0, j)
                    enter(c, 1, 1, j)
                    leave(c - 1, 0, j)
                    leave(c - 1, 1, j)
                chunk(1)
                with pe.Fori(0, 3) as j:
                    chunk(2, j)
                    chunk(3, j)
                chunk(8)
                chunk(9)
                enter(10, 0, 0)
                enter(10, 0, 1)
                transpose_h(9, 0)
                transpose_h(9, 1)
                enter(10, 1, 0)
                enter(10, 1, 1)
                transpose_h(10, 0)
                leave(9, 0)
                leave(10, 0)
                transpose_h(10, 1)
                leave(9, 1)
                pe.wait_ge(x_new, n_x_new(L, 2 * f, 0, 1))
                pe.wait_ge(hT_lo_done, n_ffn(L, f, 10, 1))
                transpose_x(L, 2 * f + 1, 0)
                leave(10, 1)

            def fill(L, name, blocks):
                n = FILLS.index(name)
                if n >= 2:
                    before = FILLS[n - 2]
                    if before in BY_DVE:
                        pe.wait_ge(tr_dve, n_of(L, BY_DVE, before))
                    else:
                        pe.wait_ge(tr_act, n_of(L, BY_ACT, before))
                else:
                    pe.wait_ge(xg_done, n_tran(L, 1, 1, n))
                for i, b in enumerate(blocks):
                    last = pe.transpose(TR[n % 2][:, i * P:(i + 1) * P], b, ident[:, :])
                last.then_inc(tr_filled, 1)

            def scores(L, r):
                t, half = divmod(r, 2)
                if r > 0:
                    pe.wait_ge(scores_biased, L * 4 + r)
                for i in range(4):
                    pair, rows_ = 2 * half + i // 2, slice((i % 2) * HD, (i % 2 + 1) * HD)
                    last = pe.matmul(acc[0][i % 2][:, (i // 2) * S:(i // 2 + 1) * S], qT[rows_, t, pair, :],
                                     kT[rows_, half, :], start=True, stop=True)
                last.then_inc(scores_ready, 1)

            def probs_T(L, r):
                pe.wait_ge(probs_ready, L * 4 + (r + 1))
                for part in range(2):
                    fill(L, f"p{r}{'ab'[part]}", [sc[:, r % 2, 2 * part + i, b * P:(b + 1) * P]
                                                  for i in range(2) for b in range(2)])

            def weighted(L, r):
                t, half = divmod(r, 2)
                pe.wait_ge(tr_act, n_of(L, BY_ACT, f"p{r}a"))
                pe.wait_ge(tr_dve, n_of(L, BY_DVE, f"p{r}b"))
                for i in range(4):
                    hh = 4 * half + i
                    for b in range(2):
                        c = ((i % 2) * 2 + b) * P
                        last = pe.matmul(U[0][:, hh * HD:(hh + 1) * HD], pT[:, i // 2, c:c + P],
                                         kv[:, b, (2 + half) * HD:(3 + half) * HD], start=(b == 0), stop=(b == 1))
                last.then_inc(pv_ready, 1)

            def spatial(L, t):
                pe.wait_ge(v_normed, L * 2 + (t + 1))
                for g in range(NG):
                    cols = slice(g * P, (g + 1) * P)
                    last = pe.matmul(U[1][:, cols], wsT[:, cols], gv[:, t, cols], start=True, stop=True)
                last.then_inc(sg_ready, 1)

            def tiles(v, t):
                return [v[:, t, i * P:(i + 1) * P] for i in range(4)]

            def mix_out_of(L, i, t):
                cols = slice(t * P, (t + 1) * P)
                return sum_out(L, POS_OUT + i, t, lambda kk: xT_hi[:, 2 * i + kk, cols],
                               lambda kk: xT_lo[:, 2 * i + kk, cols], i == 0, i == 3)

            pe.wait_ge(consts_ready, 1)
            pe.wait_ge(rows_loaded, 16 * 8)
            pe.transpose(TR[0][:, 0:NROW], rows, ident[0:NROW, 0:NROW]).then_inc(rows_T, 1)
            pe.wait_ge(gall_ready, 1)
            for t in range(2):
                pe.wait_ge(x_loaded[t], 16)
            transpose_x(0, 0, 0)
            with pe.Fori(0, DEPTH) as L:
                ffn(L, 0)
                pe.wait_ge(xT_lo_done, n_tran(L, 1, 0, 1))
                project(L, POS_KV, 0, 0, U[0][:, 0:4 * HD], 4 * HD).then_inc(proj_ready, 1)
                pe.wait_ge(x_new, n_x_new(L, 0, 1, 1))
                pe.wait_ge(xg_done, n_tran(L, 1, 0, 1))
                transpose_x(L, 1, 1)
                project(L, POS_Q, 0, 0, C0[:, :], MIX_A)
                pe.wait_ge(mix_params, L * 48 + 48)
                fill(L, "ws", [ws[:, g, :] for g in range(NG)])
                project(L, POS_Q + 1, 0, 1, C0[:, :], MIX_A).then_inc(proj_ready, 1)
                pe.wait_ge(xT_lo_done, n_tran(L, 1, 1, 1))
                project(L, POS_KV, 1, 0, U[1][:, 0:4 * HD], 4 * HD)
                pe.wait_ge(k_normed, L * 2 + 1)
                fill(L, "k0", [kd[:, 0, g, :] for g in range(2)])
                project(L, POS_Q, 1, 0, C1[:, :], MIX_A)
                pe.wait_ge(q_normed, L * 2 + 1)
                fill(L, "q0", tiles(qs, 0))
                project(L, POS_Q + 1, 1, 1, C1[:, :], MIX_A)
                pe.wait_ge(k_normed, L * 2 + 2)
                fill(L, "k1", [kd[:, 1, g, :] for g in range(2)])
                pe.wait_ge(proj_taken, n_of(L, TAKEN, "KV0"))
                project(L, POS_V, 0, 0, U[0][:, :], MIX_A)
                pe.wait_ge(proj_taken, n_of(L, TAKEN, "Q1"))
                pe.wait_ge(tr_act, n_of(L, BY_ACT, "k1"))
                scores(L, 0)
                project(L, POS_V + 1, 0, 1, U[0][:, :], MIX_A).then_inc(proj_ready, 1)
                pe.wait_ge(q_normed, L * 2 + 2)
                fill(L, "q1", tiles(qs, 1))
                scores(L, 1)
                project(L, POS_V, 1, 0, U[1][:, :], MIX_A)
                probs_T(L, 0)
                project(L, POS_V + 1, 1, 1, U[1][:, :], MIX_A)
                pe.wait_ge(proj_taken, n_of(L, TAKEN, "V0"))
                weighted(L, 0)
                pe.wait_ge(tr_act, n_of(L, BY_ACT, "q1"))
                scores(L, 2)
                project(L, POS_U, 0, 0, acc[1][0][:, :], MIX_A)
                probs_T(L, 1)
                project(L, POS_U + 1, 0, 1, acc[1][0][:, :], MIX_A).then_inc(proj_ready, 1)
                weighted(L, 1)
                scores(L, 3)
                project(L, POS_U, 1, 0, acc[1][1][:, :], MIX_A)
                pe.wait_ge(proj_taken, n_of(L, TAKEN, "V1"))
                spatial(L, 0)
                probs_T(L, 2)
                pe.wait_ge(o_done, L * 2 + 1)
                fill(L, "o0", [o[:, i * P:(i + 1) * P] for i in range(4)])
                project(L, POS_U + 1, 1, 1, acc[1][1][:, :], MIX_A)
                weighted(L, 2)
                pe.wait_ge(a_done, L * 2 + 1)
                spatial(L, 1)
                probs_T(L, 3)
                fill(L, "a0", tiles(qs, 0))
                pe.wait_ge(scores_biased, L * 4 + 4)
                pe.wait_ge(tr_dve, n_of(L, BY_DVE, "a0"))
                mix_out_of(L, 0, 0)
                weighted(L, 3)
                mix_out_of(L, 1, 0)
                pe.wait_ge(a_done, L * 2 + 2)
                fill(L, "a1", tiles(qs, 1))
                mix_out_of(L, 2, 0)
                pe.wait_ge(tr_dve, n_of(L, BY_DVE, "a1"))
                mix_out_of(L, 0, 1)
                pe.wait_ge(o_done, L * 2 + 2)
                fill(L, "o1", [o[:, i * P:(i + 1) * P] for i in range(4)])
                mix_out_of(L, 3, 0).then_inc(acc_ready, 1)
                mix_out_of(L, 1, 1)
                pe.wait_ge(tr_dve, n_of(L, BY_DVE, "o1"))
                mix_out_of(L, 2, 1)
                pe.wait_ge(x_new, n_x_new(L, 1, 0, 1))
                transpose_x(L, 2, 0)
                mix_out_of(L, 3, 1)
                ffn(L, 1)


_INS = ["x", "ffn1_norm", "ffn1_w_in", "ffn1_w_out", "mix_norm", "w_mix_in", "sgu_norm", "sgu_w", "sgu_b",
        "q_norm", "k_norm", "sink", "rel_bias", "w_mix_out", "ffn2_norm", "ffn2_w_in", "ffn2_w_out"]


def kernel(**inputs):
    import numpy as _np
    import concourse.bacc as _bacc
    from concourse import mybir as _mybir
    from concourse.bass_utils import run_bass_kernel_spmd as _run

    nc = _bacc.Bacc("TRN2", target_bir_lowering=False, num_devices=1)
    arrays, args = {}, []
    for name in _INS:
        a = _np.ascontiguousarray(inputs[name])
        arrays[f"in_{name}_dram"] = a
        args.append(nc.dram_tensor(f"in_{name}_dram", a.shape, _mybir.dt.from_np(a.dtype), kind="ExternalInput").ap())
    args.append(nc.dram_tensor("out_0_dram", arrays["in_x_dram"].shape, _mybir.dt.float32, kind="ExternalOutput").ap())
    encoder(nc, *args)
    r = _run(nc, [arrays], core_ids=[0])
    return r.results[0]["out_0_dram"]
```

```python
from contextlib import ExitStack

import numpy as np

import concourse.bass as bass
from concourse import mybir

F32 = mybir.dt.float32
F32R = mybir.dt.float32r
BF16 = mybir.dt.bfloat16
ACT = mybir.ActivationFunctionType
ALU = mybir.AluOpType
AX_X = mybir.AxisListType.X

P = 128
EPS = 1e-6
NEG_INF = -1e30
WINDOW = 128
N_BUCKETS = 32
MAX_DISTANCE = 128

SLOTS = 6
RAW = 3
UNIT = 2048
FC = 256

LAYER_POS = 78
EMPTY = 44
BIAS_AFTER = 6
LAYER_UNITS = LAYER_POS - 1
FFN_BASE = (0, 45)
POS_KV, POS_Q, POS_V, POS_U, POS_OUT = 33, 34, 36, 38, 40
OUT_TILES = (4, 6, 0, 2)
RAW_UNITS = tuple(len([p for p in range(LAYER_POS) if p % RAW == r and p != EMPTY]) for r in range(RAW))


def nth(p):
    return p if p < EMPTY else p - 1


def pos_in(f, c, u):
    return FFN_BASE[f] + (u if c == 0 else 3 * c - 1 + u)


def pos_out(f, c):
    return FFN_BASE[f] + (3 * c + 4 if c < 10 else 32)


def bucket_of(rel):
    nb = N_BUCKETS // 2
    n = np.abs(rel)
    exact = nb // 2
    large = exact + (np.log(np.maximum(n, 1).astype(np.float32) / exact)
                     / np.log(MAX_DISTANCE / exact) * (nb - exact)).astype(np.int32)
    return (rel > 0).astype(np.int32) * nb + np.where(n < exact, n, np.minimum(large, nb - 1))


def runs_of_buckets():
    rel = np.arange(-WINDOW, WINDOW + 1)
    b = bucket_of(rel)
    cuts = [0] + [i for i in range(1, len(b)) if b[i] != b[i - 1]] + [len(b)]
    return [(int(rel[a]), int(rel[z - 1]) + 1, int(b[a])) for a, z in zip(cuts, cuts[1:])]


FILLS = ["ws", "k0", "q0", "k1", "q1", "p0a", "p0b", "p1a", "p1b", "p2a", "p2b", "o0", "p3a", "p3b", "a0", "o1", "a1"]
BY_ACT = [n for n in FILLS if not n.endswith("b")]
BY_DVE = [n for n in FILLS if n.endswith("b") or n[0] in "kqoa"]
PROJ = ["KV", "Q", "V", "U"]
TAKEN = ["KV0", "Q0", "KV1", "Q1", "V0", "V1", "U0", "U1"]
NORMED = ["K0", "Q0", "K1", "Q1", "V0", "V1"]


def encoder(nc, x, ffn1_norm, ffn1_w_in, ffn1_w_out, mix_norm, w_mix_in, sgu_norm, sgu_w, sgu_b,
            q_norm, k_norm, sink, rel_bias, w_mix_out, ffn2_norm, ffn2_w_in, ffn2_w_out, out):
    _, S, D = x.shape
    DEPTH = ffn1_w_in.shape[0]
    DFF = ffn1_w_out.shape[1]
    NCH = DFF // FC
    MIX_A = sgu_norm.shape[1]
    NG = sgu_w.shape[1]
    HD = q_norm.shape[1]
    NH = sink.shape[1]
    KT = D // P
    assert S == 2 * P and NCH == 11 and D == 1024 and MIX_A == 512 and NH == 8 and HD == 64 and NG == 4

    w_in = [w.rearrange("l (k p) n -> l p k n", p=P) for w in (ffn1_w_in, ffn2_w_in)]
    w_out = [w.rearrange("l (k p) n -> l p k n", p=P) for w in (ffn1_w_out, ffn2_w_out)]
    mix_in = w_mix_in.rearrange("l (k p) n -> l p k n", p=P)
    mix_out = w_mix_out.rearrange("l (k p) n -> l p k n", p=P)
    x_tiles = x.rearrange("b (t p) d -> (b t) p d", p=P)
    out_tiles = out.rearrange("b (t p) d -> (b t) p d", p=P)
    RELS = 2 * S - 1
    bias_rows = nc.dram_tensor("bias_rows", (NH, P, RELS), F32, kind="Internal").ap()

    with ExitStack() as ctx:
        def sb(name, shape, dt=F32):
            return ctx.enter_context(nc.sbuf_tensor(name, shape, dt))

        def bank(name):
            return ctx.enter_context(nc.psum_tensor(name, [P, 512], F32))

        def sem(name):
            return ctx.enter_context(nc.semaphore(name))

        raw = sb("raw", [P, RAW, UNIT])
        w_hi = sb("w_hi", [P, SLOTS, UNIT], F32R)
        w_lo = sb("w_lo", [P, SLOTS, UNIT], F32R)
        xs = sb("xs", [P, 2, D])
        xT_hi = sb("xT_hi", [P, KT, S], F32R)
        xT_lo = sb("xT_lo", [P, KT, S], F32R)
        hT_hi = sb("hT_hi", [P, 2, 2, S], F32R)
        hT_lo = sb("hT_lo", [P, 2, 2, S], F32R)
        small = sb("small", [P, 4, FC])
        gate, h = small[:, 0:2, :], small[:, 2:4, :]
        pT = small[:, :, :].rearrange("p (a b) n -> p a (b n)", a=2)
        sc = sb("sc", [P, 2, 4, S])
        xg = sc[:, 0, :, :].rearrange("p (a b) n -> p a (b n)", a=2)
        bias = sb("bias", [P, NH, 3 * P])
        qs = sb("qs", [P, 2, MIX_A])
        kv = sb("kv", [P, 2, 4 * HD])
        kd = sb("kd", [P, 2, 2, P])
        qT_hi = sb("qT_hi", [P, 2, 4, P], F32R)
        kT_hi = sb("kT_hi", [P, 2, S], F32R)
        qT_lo = hT_lo[:, :, :, :].rearrange("p t a (b n) -> p t (a b) n", n=P)
        kT_lo = hT_hi[:, 0, :, :].rearrange("p t (g n) -> p t g n", n=P)
        gv = sb("gv", [P, 2, MIX_A])
        wsT = sb("wsT", [P, NG * P])
        o = sb("o", [P, NH * HD])
        sq = sb("sq", [P, MIX_A])
        ws = sb("ws", [P, NG, P])
        sgain = sb("sgain", [P, MIX_A])
        sinks = sb("sinks", [P, NH])
        ident = sb("ident", [P, P])
        NROW = 60
        rows = wsT[0:NROW, 0:P]
        gall = sb("gall", [P, NROW])
        gcur = sb("gcur", [P, 3 * KT + 2 + NG])
        G_Q, G_K, G_B = 3 * KT, 3 * KT + 1, 3 * KT + 2
        ms = sb("ms", [P, 2])
        inv = sb("inv", [P, 2])
        mean = sb("mean", [P, 32])
        mhalf = sb("mhalf", [P, NH])
        sums = sb("sums", [P, 32])
        rstd = sb("rstd", [P, 32])
        mx = sb("mx", [P, 2 * NH])
        nmx = sb("nmx", [P, 2 * NH])
        sd = sb("sd", [P, 2 * NH])
        den = sb("den", [P, 2 * NH])
        esink = sb("esink", [P, 2 * NH])
        dtot = sb("dtot", [P, 2 * NH])
        rden = sb("rden", [P, 2 * NH])
        rb = sb("rb", [NH, N_BUCKETS])
        brow = o[0:NH, 0:RELS]

        U = [bank("U0"), bank("U1")]
        acc = [[bank("C0"), bank("C1")], [bank("D0"), bank("D1")]]
        C0, C1 = acc[0]
        TR = [bank("TR0"), bank("TR1")]
        PROJ_BANK = {"KV0": U[0], "KV1": U[1], "Q0": C0, "Q1": C1, "V0": U[0], "V1": U[1],
                     "U0": acc[1][0], "U1": U[0]}
        PV, SG = acc[1][1], U[1]

        x_loaded = [sem("x_loaded0"), sem("x_loaded1")]
        gain_loaded = sem("gain_loaded")
        rows_loaded = sem("rows_loaded")
        head_rows_loaded = sem("head_rows_loaded")
        rb_loaded = sem("rb_loaded")
        bias_stored = sem("bias_stored")
        bias_loaded = sem("bias_loaded")
        mix_params = sem("mix_params")
        consts_ready = sem("consts_ready")
        rows_T = sem("rows_T")
        gain_taken = sem("gain_taken")
        half_hi = sem("half_hi")
        half_lo = sem("half_lo")
        unit_loaded = [sem(f"unit_loaded{r}") for r in range(RAW)]
        hi_ready = sem("hi_ready")
        lo_ready = sem("lo_ready")
        units_used = sem("units_used")
        gu_ready = sem("gu_ready")
        silu_done = sem("silu_done")
        h_done = sem("h_done")
        hT_psum = sem("hT_psum")
        hT_hi_done = sem("hT_hi_done")
        hT_lo_done = sem("hT_lo_done")
        acc_ready = sem("acc_ready")
        half_sum = sem("half_sum")
        x_new = sem("x_new")
        xT_psum = sem("xT_psum")
        xg_done = sem("xg_done")
        xT_hi_done = sem("xT_hi_done")
        xT_lo_done = sem("xT_lo_done")
        ms_done = sem("ms_done")
        inv_done = sem("inv_done")
        proj_ready = sem("proj_ready")
        proj_taken = sem("proj_taken")
        sq_done = sem("sq_done")
        sums_done = sem("sums_done")
        rstd_done = sem("rstd_done")
        k_normed = sem("k_normed")
        q_normed = sem("q_normed")
        v_normed = sem("v_normed")
        tr_filled = sem("tr_filled")
        tr_act = sem("tr_act")
        tr_dve = sem("tr_dve")
        scores_ready = sem("scores_ready")
        scores_biased = sem("scores_biased")
        probs_ready = sem("probs_ready")
        pv_ready = sem("pv_ready")
        o_done = sem("o_done")
        sg_ready = sem("sg_ready")
        a_done = sem("a_done")
        pool_step = sem("pool_step")
        dve_step = sem("dve_step")
        stored = sem("stored")
        turns_sp, turns_pool, turns_dve = sem("turns_sp"), sem("turns_pool"), sem("turns_dve")

        def n_unit(L, p, j=0):
            return L * LAYER_UNITS + j * 6 + (nth(p) + 1)

        def n_used(L, p, j=0):
            return L * LAYER_UNITS + j * 6 + (SLOTS + nth(p) + 1)

        def n_slot_free(L, p, j=0):
            if p < SLOTS:
                return L * LAYER_UNITS + (p + 1)
            return n_used(L, p - SLOTS if p - SLOTS != EMPTY else p - 2 * SLOTS, j)

        def n_raw_free(L, p, j=0):
            if p < RAW:
                return L * LAYER_UNITS + (p + 1)
            q = p - RAW if p - RAW != EMPTY else p - 2 * RAW
            return L * LAYER_UNITS + j * 6 + (RAW + nth(q) + 1)

        def n_loaded(L, p, j=0):
            k = p // RAW - (1 if p > EMPTY and p % RAW == EMPTY % RAW else 0)
            return L * (32 * RAW_UNITS[p % RAW]) + j * 64 + 32 * (k + 1)

        def n_ffn(L, f, c, t, j=0):
            return L * (4 * NCH) + j * 4 + (2 * NCH * f + 2 * c + t + 1)

        def n_gu(L, f, c, j=0):
            return L * (2 * NCH) + j * 2 + (NCH * f + c + 1)

        def n_tran(L, q, t, half):
            return L * 12 + (4 * q + 2 * t + half + 1)

        def n_x_new(L, ph, t, half):
            return L * 12 + (4 * (ph + 1) + 2 * t + half + 1)

        def n_inv(L, q, t):
            return L * 6 + (2 * q + t + 1)

        def n_of(L, names, name):
            return L * len(names) + (names.index(name) + 1)

        block = ctx.enter_context(nc.Block())

        @block.sync
        def _(sp):
            def load(L, p, parts, j=0):
                sp.wait_ge(lo_ready, n_raw_free(L, p, j))
                sp.sem_inc(turns_sp, 1)
                dst = raw[:, p % RAW, :]
                for d, s in parts(dst):
                    sp.dma_start(d, s).then_inc(unit_loaded[p % RAW], 16)

            def load_in(L, f, c, u, j=0):
                def parts(dst):
                    d = dst.rearrange("p (k g n) -> p k g n", k=4, g=2)
                    for g in range(2):
                        cols = bass.ds(j * (2 * FC) + (g * DFF + c * FC), FC)
                        yield d[:, :, g, :], w_in[f][bass.ds(L, 1), :, 4 * u:4 * u + 4, cols][0]
                load(L, pos_in(f, c, u), parts, j)

            def load_out(L, f, c, j=0):
                def parts(dst):
                    for kk in range(2):
                        yield (dst[:, kk * D:(kk + 1) * D],
                               w_out[f][bass.ds(L, 1), :, bass.ds(j * 4 + (2 * c + kk), 1), :][0, :, 0, :])
                load(L, pos_out(f, c), parts, j)

            def load_mix(L, p, col, width, k0):
                def parts(dst):
                    n = UNIT // width // 2
                    d = dst.rearrange("p (k n) -> p k n", n=width)
                    for i in range(2):
                        yield (d[:, i * n:(i + 1) * n, :],
                               mix_in[bass.ds(L, 1), :, k0 + i * n:k0 + (i + 1) * n, col:col + width][0])
                load(L, p, parts)

            def load_mix_out(L, i):
                def parts(dst):
                    for kk in range(2):
                        yield dst[:, kk * D:(kk + 1) * D], mix_out[bass.ds(L, 1), :, OUT_TILES[i] + kk, :][0]
                load(L, POS_OUT + i, parts)

            def ffn_weights(L, f):
                def chunk(c, j=0):
                    load_in(L, f, c + 1, 0, j)
                    load_in(L, f, c + 1, 1, j)
                    load_out(L, f, c, j)
                chunk(0)
                with sp.Fori(0, 4) as j:
                    chunk(1, j)
                    chunk(2, j)
                chunk(9)
                load_out(L, f, 10)

            sp.dma_start(xs[:, 0, :], x_tiles[0]).then_inc(x_loaded[0], 16)
            load_in(0, 0, 0, 0)
            load_in(0, 0, 0, 1)
            sp.dma_start(xs[:, 1, :], x_tiles[1]).then_inc(x_loaded[1], 16)
            with sp.Fori(0, DEPTH) as L:
                ffn_weights(L, 0)
                load_mix(L, POS_KV, 3 * MIX_A, 4 * HD, 0)
                for i, (p, col) in enumerate([(POS_Q, 2 * MIX_A), (POS_V, MIX_A), (POS_U, 0)]):
                    for u in range(2):
                        load_mix(L, p + u, col, MIX_A, 4 * u)
                for i in range(4):
                    load_mix_out(L, i)
                for u in range(2):
                    load_in(L, 1, 0, u)
                ffn_weights(L, 1)
                with sp.If(L < DEPTH - 1):
                    ahead = nc.s_assert_within(L + 1, 1, DEPTH - 1,
                                               skip_runtime_bounds_check_because="the branch is taken below the last layer")
                    for u in range(2):
                        load_in(ahead, 0, 0, u)
            for t in range(2):
                for half in range(2):
                    sp.wait_ge(x_new, n_x_new(DEPTH - 1, 2, t, half))
                    cols = slice(half * 512, (half + 1) * 512)
                    sp.dma_start(out_tiles[t][:, cols], xs[:, t, cols]).then_inc(stored, 16)
            sp.wait_ge(stored, 64)

        @block.gpsimd
        def _(pool):
            steps = 0

            def step(ins, L=0, count=True):
                nonlocal steps
                steps += 1
                ins.then_inc(pool_step, 1)
                pool.wait_ge(pool_step, L * per_layer + steps)

            per_layer = 0
            step(pool.memset(ident[:, :], 0.0))
            step(pool.affine_select(out=ident[:, :], in_=ident[:, :], compare_op=ALU.not_equal, fill=1.0,
                                    base=0, pattern=[[-1, P]], channel_multiplier=1))
            pool.memset(mhalf[:, :], -0.5).then_inc(consts_ready, 1)
            for r0, v in ((48, q_norm), (50, k_norm)):
                pool.dma_start(rows[r0:r0 + 2, :].rearrange("l (a d) -> l a d", a=2),
                               v.unsqueeze(1).to_broadcast([DEPTH, 2, HD])).then_inc(head_rows_loaded, 16)
            pool.dma_start(rows[52:60, :], sgu_b.rearrange("l g p -> (l g) p")).then_inc(head_rows_loaded, 16)
            step(pool.memset(brow, NEG_INF))
            pool.wait_ge(rb_loaded, 16)
            zero = WINDOW + P - 1
            for a, z, b in runs_of_buckets():
                last = pool.tensor_copy(brow[:, zero + a:zero + z], rb[:, b:b + 1].to_broadcast([NH, z - a]))
            step(last)

            def rsqrt(L, dst, src, tmp, n, width):
                pool.sem_inc(turns_pool, 1)
                step(pool.tensor_scalar(tmp, src, 1.0 / n, EPS, ALU.mult, ALU.add), L)
                return pool.tensor_tensor(dst, tmp, mhalf[:, 0:width], ALU.pow)

            def inverse_rms(L, q, t):
                pool.wait_ge(ms_done, n_inv(L, q, t))
                rsqrt(L, inv[:, t:t + 1], ms[:, t:t + 1], mean[:, 30 + t:31 + t], D, 1).then_inc(inv_done, 1)

            def squares(L, name, src, n):
                if name != "K0":
                    pool.wait_ge(sums_done, n_of(L, NORMED, NORMED[NORMED.index(name) - 1]))
                pool.wait_ge(proj_taken, n_of(L, TAKEN, name.replace("K", "KV")))
                pool.tensor_tensor(sq[:, 0:n], src, src, ALU.mult).then_inc(sq_done, 1)

            def norm(L, name, c0, groups, n):
                pool.wait_ge(sums_done, n_of(L, NORMED, name))
                return rsqrt(L, rstd[:, c0:c0 + groups], sums[:, c0:c0 + groups], mean[:, c0:c0 + groups], n, groups)

            base = steps
            inverse_rms(0, 0, 0)
            inverse_rms(0, 0, 1)
            pool.wait_ge(units_used, n_used(0, BIAS_AFTER))
            pool.dma_start(bias_rows, brow.unsqueeze(1).to_broadcast([NH, P, RELS])).then_inc(bias_stored, 16)
            pool.wait_ge(bias_stored, 16)
            for hh in range(NH):
                src = bass.AP(bias_rows.tensor, hh * P * RELS + (P - 1), [[RELS - 1, P], [1, 3 * P]])
                pool.dma_start(bias[:, hh, :], src).then_inc(bias_loaded, 16)
            per_layer = 6 + 2 + 4 + 6
            first = steps
            with pool.Fori(0, DEPTH) as L:
                pool.wait_ge(units_used, L * LAYER_UNITS + SLOTS)
                pool.dma_start(ws[:, :, :], sgu_w.rearrange("l g p q -> l p g q")[bass.ds(L, 1)][0]).then_inc(mix_params, 16)
                pool.dma_start(sgain[:, :], sgu_norm[bass.ds(L, 1), :].partition_broadcast(P)[:, 0, :]).then_inc(mix_params, 16)
                pool.dma_start(sinks[:, :], sink[bass.ds(L, 1), :].partition_broadcast(P)[:, 0, :]).then_inc(mix_params, 16)
                inverse_rms(L, 1, 0)
                inverse_rms(L, 1, 1)
                for t in range(2):
                    squares(L, f"K{t}", kv[:, t, 0:2 * HD], 2 * HD)
                    norm(L, f"K{t}", 2 * t, 2, HD).then_inc(rstd_done, 1)
                    squares(L, f"Q{t}", qs[:, t, :], MIX_A)
                    step(norm(L, f"Q{t}", 4 + 8 * t, NH, HD), L)
                    qv = qs[:, t, :].rearrange("p (h d) -> p h d", h=NH)
                    pool.tensor_tensor(qv, qv, rstd[:, 4 + 8 * t:12 + 8 * t].unsqueeze(2).to_broadcast([P, NH, HD]),
                                       ALU.mult).then_inc(q_normed, 1)
                pool.wait_ge(mix_params, L * 48 + 48)
                for t in range(2):
                    squares(L, f"V{t}", gv[:, t, :], MIX_A)
                    step(norm(L, f"V{t}", 20 + 4 * t, NG, P), L)
                    vv = gv[:, t, :].rearrange("p (g d) -> p g d", g=NG)
                    step(pool.tensor_tensor(vv, vv, rstd[:, 20 + 4 * t:24 + 4 * t].unsqueeze(2).to_broadcast([P, NG, P]),
                                            ALU.mult), L)
                    pool.tensor_tensor(gv[:, t, :], gv[:, t, :], sgain[:, :], ALU.mult).then_inc(v_normed, 1)
                for q in (2, 3):
                    inverse_rms(L, q, 0)
                    inverse_rms(L, q, 1)
                assert steps - first == per_layer, steps - first

        @block.scalar
        def _(act):
            def split(L, p, j=0):
                act.wait_ge(unit_loaded[p % RAW], n_loaded(L, p, j))
                act.wait_ge(units_used, n_slot_free(L, p, j))
                a = 0
                if p < 2:
                    a = UNIT // 2
                    act.activation(w_hi[:, p, 0:a], raw[:, p, 0:a], ACT.Copy).then_inc(half_hi, 1)
                act.activation(w_hi[:, p % SLOTS, a:], raw[:, p % RAW, a:], ACT.Copy).then_inc(hi_ready, 1)

            def silu(L, f, c, t, j=0):
                if t == 0:
                    act.wait_ge(gu_ready, n_gu(L, f, c, j))
                else:
                    act.wait_ge(units_used, n_used(L, pos_in(f, c, 1), j))
                if c == 0:
                    act.wait_ge(inv_done, n_inv(L, 2 * f, t))
                else:
                    act.wait_ge(h_done, n_ffn(L, f, c - 1, t, j))
                act.activation(gate[:, t, :], U[t][:, 0:FC], ACT.Silu, scale=inv[:, t:t + 1]).then_inc(silu_done, 1)

            def take_hT(L, f, c, t, j=0):
                act.wait_ge(hT_psum, n_ffn(L, f, c, t, j))
                act.activation(hT_hi[:, c % 2, :, t * P:(t + 1) * P],
                               TR[t][:, 0:FC].rearrange("p (k n) -> p k n", k=2), ACT.Copy).then_inc(hT_hi_done, 1)

            def sum_squares(L, ph, t):
                if ph < 0:
                    act.wait_ge(x_loaded[t], 16)
                else:
                    act.wait_ge(x_new, n_x_new(L, ph, t, 1))
                if ph >= 0 or t == 1:
                    act.wait_ge(ms_done, n_inv(L, ph + 1, t) - 1)
                act.activation(sq[:, :].bitcast(BF16), xs[:, t, :], ACT.Square, accum_out=ms[:, t:t + 1]).then_inc(ms_done, 1)

            def take_xT(L, q, t):
                for half in range(2):
                    act.wait_ge(xg_done, n_tran(L, q, t, half))
                    act.activation(xT_hi[:, 4 * half:4 * half + 4, t * P:(t + 1) * P],
                                   xg[:, half, :].rearrange("p (k n) -> p k n", k=4), ACT.Copy).then_inc(xT_hi_done, 1)

            def ffn(L, f, after):
                def chunk(c, j=0):
                    if c > 0:
                        silu(L, f, c - 1, 1, j)
                    split(L, pos_in(f, c + 1, 0), j)
                    if c > 0:
                        take_hT(L, f, c - 1, 0, j)
                        take_hT(L, f, c - 1, 1, j)
                    silu(L, f, c, 0, j)
                    split(L, pos_in(f, c + 1, 1), j)
                    split(L, pos_out(f, c), j)
                chunk(0)
                with act.Fori(0, 4) as j:
                    chunk(1, j)
                    chunk(2, j)
                chunk(9)
                silu(L, f, 9, 1)
                split(L, pos_out(f, 10))
                take_hT(L, f, 9, 0)
                take_hT(L, f, 9, 1)
                silu(L, f, 10, 0)
                if after is not None:
                    split(L, after[0])
                silu(L, f, 10, 1)
                take_hT(L, f, 10, 0)
                if after is None:
                    with act.If(L < DEPTH - 1):
                        split(L + 1, 0)
                        split(L + 1, 1)
                else:
                    split(L, after[1])
                take_hT(L, f, 10, 1)
                sum_squares(L, 2 * f, 0)
                if after is None:
                    with act.If(L < DEPTH - 1):
                        take_xT(L, 3, 0)
                else:
                    take_xT(L, 1, 0)
                    split(L, after[2])
                sum_squares(L, 2 * f, 1)

            def take(L, name, dst, func, width):
                t = int(name[-1])
                if t == 0:
                    act.wait_ge(proj_ready, n_of(L, PROJ, name[:-1]))
                else:
                    last = {"KV": POS_KV, "Q": POS_Q + 1, "V": POS_V + 1, "U": POS_U + 1}[name[:-1]]
                    act.wait_ge(units_used, n_used(L, last))
                if name[:-1] == "KV":
                    act.wait_ge(inv_done, n_inv(L, 1, t))
                act.activation(dst, PROJ_BANK[name][:, 0:width], func, scale=inv[:, t:t + 1]).then_inc(proj_taken, 1)

            def evacuate(L, name, dst, width=512, scale=1.0):
                n = FILLS.index(name)
                act.wait_ge(tr_filled, n_of(L, FILLS, name))
                src = TR[n % 2][:, 0:width]
                if len(dst.shape) == 3:
                    src = src.rearrange("p (k n) -> p k n", k=dst.shape[1])
                act.activation(dst, src, ACT.Copy, scale=scale).then_inc(tr_act, 1)

            def exps(L, r):
                t, half = divmod(r, 2)
                act.wait_ge(scores_biased, L * 4 + (r + 1))
                for i in range(4):
                    c = t * NH + 4 * half + i
                    act.activation(sc[:, r % 2, i, :], sc[:, r % 2, i, :], ACT.Exp, bias=nmx[:, c:c + 1],
                                   accum_out=den[:, c:c + 1])
                c = t * NH + 4 * half
                act.activation(esink[:, c:c + 4], sd[:, c:c + 4], ACT.Exp).then_inc(probs_ready, 1)

            act.dma_start(rows[0:2 * KT, :], ffn1_norm.rearrange("l (k p) -> (l k) p", p=P)).then_inc(gain_loaded, 16)
            with nc.allow_non_contiguous_dma(reason="256 numbers, once"):
                act.dma_start(rb[:, :], rel_bias.rearrange("b h -> h b")).then_inc(rb_loaded, 16)
            for r0, v in ((16, mix_norm), (32, ffn2_norm)):
                act.dma_start(rows[r0:r0 + 2 * KT, :], v.rearrange("l (k p) -> (l k) p", p=P)).then_inc(rows_loaded, 16)
            take_xT(0, 0, 0)
            split(0, 0)
            sum_squares(0, -1, 0)
            split(0, 1)
            sum_squares(0, -1, 1)
            with act.Fori(0, DEPTH) as L:
                take_xT(L, 0, 1)
                ffn(L, 0, [POS_KV, POS_Q, POS_Q + 1])
                take_xT(L, 1, 1)
                take(L, "KV0", kv[:, 0, :], ACT.Copy, 4 * HD)
                split(L, POS_V)
                take(L, "Q0", qs[:, 0, :], ACT.Copy, MIX_A)
                evacuate(L, "ws", wsT[:, :])
                split(L, POS_V + 1)
                take(L, "KV1", kv[:, 1, :], ACT.Copy, 4 * HD)
                split(L, POS_U)
                evacuate(L, "k0", kT_hi[:, :, 0:P], 2 * P, gcur[:, G_K:G_K + 1])
                take(L, "Q1", qs[:, 1, :], ACT.Copy, MIX_A)
                evacuate(L, "q0", qT_hi[:, 0, :, :], 512, gcur[:, G_Q:G_Q + 1])
                split(L, POS_U + 1)
                evacuate(L, "k1", kT_hi[:, :, P:2 * P], 2 * P, gcur[:, G_K:G_K + 1])
                evacuate(L, "q1", qT_hi[:, 1, :, :], 512, gcur[:, G_Q:G_Q + 1])
                split(L, POS_OUT)
                exps(L, 0)
                evacuate(L, "p0a", pT[:, 0, :])
                exps(L, 1)
                take(L, "V0", gv[:, 0, :], ACT.Gelu_apprx_tanh, MIX_A)
                take(L, "V1", gv[:, 1, :], ACT.Gelu_apprx_tanh, MIX_A)
                exps(L, 2)
                evacuate(L, "p1a", pT[:, 0, :])
                split(L, POS_OUT + 1)
                exps(L, 3)
                evacuate(L, "p2a", pT[:, 0, :])
                take(L, "U0", qs[:, 0, :], ACT.Gelu_apprx_tanh, MIX_A)
                evacuate(L, "o0", xT_hi[:, 4:8, 0:P])
                evacuate(L, "p3a", pT[:, 0, :])
                split(L, POS_OUT + 2)
                take(L, "U1", qs[:, 1, :], ACT.Gelu_apprx_tanh, MIX_A)
                evacuate(L, "a0", xT_hi[:, 0:4, 0:P])
                evacuate(L, "o1", xT_hi[:, 4:8, P:2 * P])
                split(L, POS_OUT + 3)
                evacuate(L, "a1", xT_hi[:, 0:4, P:2 * P])
                split(L, FFN_BASE[1])
                split(L, FFN_BASE[1] + 1)
                sum_squares(L, 1, 0)
                take_xT(L, 2, 0)
                sum_squares(L, 1, 1)
                take_xT(L, 2, 1)
                ffn(L, 1, None)

        @block.vector
        def _(dve):
            steps = 0
            per_layer = 0

            def step(ins, L=0):
                nonlocal steps
                steps += 1
                ins.then_inc(dve_step, 1)
                dve.wait_ge(dve_step, L * per_layer + steps)

            def split(L, p, j=0):
                a = 0
                if p < 2:
                    a = UNIT // 2
                    dve.wait_ge(half_hi, L * 2 + (p + 1))
                    dve.tensor_tensor(w_lo[:, p, 0:a], raw[:, p, 0:a], w_hi[:, p, 0:a].bitcast(F32),
                                      ALU.subtract).then_inc(half_lo, 1)
                dve.wait_ge(hi_ready, n_unit(L, p, j))
                dve.tensor_tensor(w_lo[:, p % SLOTS, a:], raw[:, p % RAW, a:], w_hi[:, p % SLOTS, a:].bitcast(F32),
                                  ALU.subtract).then_inc(lo_ready, 1)

            def mul(L, f, c, t, j=0):
                dve.wait_ge(silu_done, n_ffn(L, f, c, t, j))
                dve.scalar_tensor_tensor(out=h[:, t, :], in0=U[t][:, FC:2 * FC], scalar=inv[:, t:t + 1],
                                         in1=gate[:, t, :], op0=ALU.mult, op1=ALU.mult).then_inc(h_done, 1)

            def take_hT(L, f, c, t, j=0):
                dve.wait_ge(hT_hi_done, n_ffn(L, f, c, t, j))
                cols = slice(t * P, (t + 1) * P)
                dve.tensor_tensor(hT_lo[:, c % 2, :, cols], TR[t][:, 0:FC].rearrange("p (k n) -> p k n", k=2),
                                  hT_hi[:, c % 2, :, cols].bitcast(F32), ALU.subtract).then_inc(hT_lo_done, 1)

            def residual(L, ph, t):
                if t == 0:
                    dve.wait_ge(acc_ready, L * 3 + (ph + 1))
                elif ph == 1:
                    dve.wait_ge(units_used, n_used(L, POS_OUT + 3))
                else:
                    dve.wait_ge(half_sum, L * 2 + (ph // 2 + 1))
                for half in range(2):
                    if t == 1 and half == 1 and ph != 1:
                        dve.wait_ge(units_used, n_used(L, pos_out(ph // 2, 10)))
                        dve.sem_inc(turns_dve, 1)
                    xh = xs[:, t, half * 512:(half + 1) * 512]
                    dve.scalar_tensor_tensor(out=xh, in0=acc[t][half][:, :], scalar=1.0 if ph == 1 else 0.5, in1=xh,
                                             op0=ALU.mult, op1=ALU.add).then_inc(x_new, 1)

            def take_xT(L, q, t):
                g0 = {0: 2 * KT, 1: 0, 2: KT, 3: 2 * KT}[q]
                for half in range(2):
                    dve.wait_ge(xT_psum, n_tran(L, q, t, half))
                    gain = gcur[:, g0 + 4 * half:g0 + 4 * half + 4].unsqueeze(2).to_broadcast([P, 4, P])
                    dve.tensor_tensor(xg[:, half, :].rearrange("p (k n) -> p k n", k=4),
                                      TR[half][:, :].rearrange("p (k n) -> p k n", k=4), gain, ALU.mult).then_inc(xg_done, 1)
                for half in range(2):
                    dve.wait_ge(xT_hi_done, n_tran(L, q, t, half))
                    ks, cols = slice(4 * half, 4 * half + 4), slice(t * P, (t + 1) * P)
                    dve.tensor_tensor(xT_lo[:, ks, cols], xg[:, half, :].rearrange("p (k n) -> p k n", k=4),
                                      xT_hi[:, ks, cols].bitcast(F32), ALU.subtract).then_inc(xT_lo_done, 1)

            def layer_gains(L):
                for c, src in ((0, 2 * KT), (KT, 4 * KT), (2 * KT, KT)):
                    dve.tensor_copy(gcur[:, c:c + KT], gall[:, bass.ds(L * KT + src, KT)])
                dve.tensor_scalar(gcur[:, G_Q:G_Q + 1], gall[:, bass.ds(L + 48, 1)], float(HD) ** -0.5, None, ALU.mult)
                dve.tensor_copy(gcur[:, G_K:G_K + 1], gall[:, bass.ds(L + 50, 1)])
                step(dve.tensor_copy(gcur[:, G_B:G_B + NG], gall[:, bass.ds(L * NG + 52, NG)]), L)

            def ffn(L, f, after):
                def chunk(c, j=0):
                    if c > 0:
                        mul(L, f, c - 1, 1, j)
                    split(L, pos_in(f, c + 1, 0), j)
                    if c > 0:
                        take_hT(L, f, c - 1, 0, j)
                        take_hT(L, f, c - 1, 1, j)
                    else:
                        dve.wait_ge(inv_done, n_inv(L, 2 * f, 1))
                    mul(L, f, c, 0, j)
                    split(L, pos_in(f, c + 1, 1), j)
                    split(L, pos_out(f, c), j)
                chunk(0)
                with dve.Fori(0, 4) as j:
                    chunk(1, j)
                    chunk(2, j)
                if f == 0:
                    layer_gains(L)
                chunk(9)
                mul(L, f, 9, 1)
                split(L, pos_out(f, 10))
                take_hT(L, f, 9, 0)
                take_hT(L, f, 9, 1)
                mul(L, f, 10, 0)
                if after is not None:
                    split(L, after[0])
                mul(L, f, 10, 1)
                take_hT(L, f, 10, 0)
                if after is None:
                    with dve.If(L < DEPTH - 1):
                        split(L + 1, 0)
                        split(L + 1, 1)
                else:
                    split(L, after[1])
                take_hT(L, f, 10, 1)
                residual(L, 2 * f, 0)
                if after is None:
                    with dve.If(L < DEPTH - 1):
                        take_xT(L, 3, 0)
                else:
                    take_xT(L, 1, 0)
                residual(L, 2 * f, 1)
                if after is not None:
                    split(L, after[2])

            def sum_of(L, name, c0, groups, n):
                dve.wait_ge(sq_done, n_of(L, NORMED, name))
                dve.tensor_reduce(sums[:, c0:c0 + groups], sq[:, 0:groups * n].rearrange("p (g n) -> p g n", g=groups),
                                  AX_X, ALU.add).then_inc(sums_done, 1)

            def scale_k(L, t):
                dve.wait_ge(rstd_done, L * 2 + (t + 1))
                for g in range(2):
                    last = dve.tensor_scalar(kd[:, t, g, :].rearrange("p (a d) -> p a d", a=2),
                                             kv[:, t, g * HD:(g + 1) * HD].unsqueeze(1).to_broadcast([P, 2, HD]),
                                             rstd[:, 2 * t + g:2 * t + g + 1], None, ALU.mult)
                last.then_inc(k_normed, 1)

            def biased(L, r):
                t, half = divmod(r, 2)
                dve.wait_ge(scores_ready, L * 4 + (r + 1))
                dve.sem_inc(turns_dve, 1)
                for i in range(4):
                    hh = 4 * half + i
                    c = t * NH + hh
                    ins = dve.tensor_tensor_reduce(
                        sc[:, r % 2, i, :], acc[0][i % 2][:, (i // 2) * S:(i // 2 + 1) * S],
                        bias[:, hh, (1 - t) * P:(1 - t) * P + S], 1.0, sinks[:, hh:hh + 1],
                        ALU.add, ALU.max, mx[:, c:c + 1])
                step(ins, L)
                c = t * NH + 4 * half
                dve.tensor_scalar(nmx[:, c:c + 4], mx[:, c:c + 4], -1.0, None, ALU.mult)
                dve.tensor_tensor(sd[:, c:c + 4], sinks[:, 4 * half:4 * half + 4], mx[:, c:c + 4],
                                  ALU.subtract).then_inc(scores_biased, 1)

            def evacuate(L, name, dst, src_hi=None):
                n = FILLS.index(name)
                if src_hi is None:
                    dve.wait_ge(tr_filled, n_of(L, FILLS, name))
                    dve.tensor_copy(dst, TR[n % 2][:, :]).then_inc(tr_dve, 1)
                else:
                    dve.wait_ge(tr_act, n_of(L, BY_ACT, name))
                    dve.tensor_tensor(dst, TR[n % 2][:, :].rearrange("p (k n) -> p k n", k=4), src_hi.bitcast(F32),
                                      ALU.subtract).then_inc(tr_dve, 1)

            def evacuate_lo(L, name, dst, hi, gain):
                n = FILLS.index(name)
                dve.wait_ge(tr_act, n_of(L, BY_ACT, name))
                dve.scalar_tensor_tensor(out=dst, in0=TR[n % 2][:, 0:dst.shape[1] * P].rearrange("p (k n) -> p k n", n=P),
                                         scalar=gain, in1=hi.bitcast(F32), op0=ALU.mult, op1=ALU.subtract
                                         ).then_inc(tr_dve, 1)

            def attended(L, t):
                cs = slice(t * NH, (t + 1) * NH)
                dve.wait_ge(probs_ready, L * 4 + (2 * t + 2))
                step(dve.tensor_tensor(dtot[:, cs], den[:, cs], esink[:, cs], ALU.add), L)
                step(dve.reciprocal(rden[:, cs], dtot[:, cs]), L)
                dve.wait_ge(pv_ready, L * 4 + (2 * t + 2))
                dve.tensor_tensor(o[:, :].rearrange("p (h d) -> p h d", h=NH),
                                  PV[:, :].rearrange("p (h d) -> p h d", h=NH),
                                  rden[:, cs].unsqueeze(2).to_broadcast([P, NH, HD]), ALU.mult).then_inc(o_done, 1)

            def gated(L, t):
                dve.wait_ge(sg_ready, L * 2 + (t + 1))
                dve.wait_ge(proj_taken, n_of(L, TAKEN, f"U{t}"))
                for g in range(NG):
                    cols = slice(g * P, (g + 1) * P)
                    last = dve.scalar_tensor_tensor(out=qs[:, t, cols], in0=SG[:, cols], scalar=gcur[:, G_B + g:G_B + g + 1],
                                                    in1=qs[:, t, cols], op0=ALU.add, op1=ALU.mult)
                last.then_inc(a_done, 1)

            dve.sem_inc(x_new, 4)
            dve.memset(mx[:, :], 0.0).then_inc(units_used, SLOTS)
            dve.sem_inc(lo_ready, RAW)
            dve.wait_ge(rows_T, 1)
            step(dve.tensor_copy(gall[:, 0:2 * KT], C0[:, 0:2 * KT]))
            step(dve.tensor_copy(gcur[:, 2 * KT:3 * KT], gall[:, 0:KT]))
            dve.sem_inc(gain_taken, 1)
            take_xT(0, 0, 0)
            split(0, 0)
            dve.wait_ge(rows_T, 2)
            step(dve.tensor_copy(gall[:, 2 * KT:NROW], C0[:, 2 * KT:NROW]))
            split(0, 1)

            first = steps
            per_layer = 1 + 4 + 4
            with dve.Fori(0, DEPTH) as L:
                take_xT(L, 0, 1)
                ffn(L, 0, [POS_KV, POS_Q, POS_Q + 1])
                take_xT(L, 1, 1)
                sum_of(L, "K0", 0, 2, HD)
                split(L, POS_V)
                scale_k(L, 0)
                sum_of(L, "Q0", 4, NH, HD)
                split(L, POS_V + 1)
                evacuate_lo(L, "k0", kT_lo[:, 0, :, :], kT_hi[:, :, 0:P], gcur[:, G_K:G_K + 1])
                sum_of(L, "K1", 2, 2, HD)
                split(L, POS_U)
                scale_k(L, 1)
                evacuate_lo(L, "q0", qT_lo[:, 0, :, :], qT_hi[:, 0, :, :], gcur[:, G_Q:G_Q + 1])
                sum_of(L, "Q1", 12, NH, HD)
                evacuate_lo(L, "k1", kT_lo[:, 1, :, :], kT_hi[:, :, P:2 * P], gcur[:, G_K:G_K + 1])
                split(L, POS_U + 1)
                evacuate_lo(L, "q1", qT_lo[:, 1, :, :], qT_hi[:, 1, :, :], gcur[:, G_Q:G_Q + 1])
                dve.wait_ge(mix_params, L * 48 + 48)
                dve.wait_ge(bias_loaded, 16 * NH)
                biased(L, 0)
                split(L, POS_OUT)
                biased(L, 1)
                evacuate(L, "p0b", pT[:, 1, :])
                biased(L, 2)
                sum_of(L, "V0", 20, NG, P)
                evacuate(L, "p1b", pT[:, 1, :])
                biased(L, 3)
                sum_of(L, "V1", 24, NG, P)
                attended(L, 0)
                evacuate(L, "p2b", pT[:, 1, :])
                split(L, POS_OUT + 1)
                gated(L, 0)
                evacuate(L, "o0", xT_lo[:, 4:8, 0:P], xT_hi[:, 4:8, 0:P])
                evacuate(L, "p3b", pT[:, 1, :])
                split(L, POS_OUT + 2)
                evacuate(L, "a0", xT_lo[:, 0:4, 0:P], xT_hi[:, 0:4, 0:P])
                attended(L, 1)
                gated(L, 1)
                evacuate(L, "o1", xT_lo[:, 4:8, P:2 * P], xT_hi[:, 4:8, P:2 * P])
                split(L, POS_OUT + 3)
                evacuate(L, "a1", xT_lo[:, 0:4, P:2 * P], xT_hi[:, 0:4, P:2 * P])
                split(L, FFN_BASE[1])
                residual(L, 1, 0)
                split(L, FFN_BASE[1] + 1)
                take_xT(L, 2, 0)
                residual(L, 1, 1)
                take_xT(L, 2, 1)
                ffn(L, 1, None)
                assert steps - first == per_layer, steps - first

        @block.tensor
        def _(pe):
            def split_ready(L, p, j=0):
                pe.wait_ge(lo_ready, L * LAYER_UNITS + j * 6 + (RAW + nth(p) + 1))

            def products(outs, x_hi, x_lo, slot, cols, start, stop):
                for out_, c in zip(outs, cols):
                    pe.matmul(out_, x_hi, w_hi[:, slot, c], start=start, stop=False)
                    pe.matmul(out_, x_hi, w_lo[:, slot, c], start=False, stop=False)
                for out_, c in zip(outs, cols):
                    last = pe.matmul(out_, x_lo, w_hi[:, slot, c], start=False, stop=stop)
                return last

            def project(L, p, t, u, dst, width, j=0):
                if p < 2:
                    pe.wait_ge(half_lo, L * 2 + (p + 1))
                else:
                    split_ready(L, p, j)
                n = UNIT // width
                for kk in range(n):
                    if p < 2 and kk == n // 2:
                        split_ready(L, p, j)
                    k = n * u + kk
                    last = products([dst], xT_hi[:, k, t * P:(t + 1) * P], xT_lo[:, k, t * P:(t + 1) * P], p % SLOTS,
                                    [slice(kk * width, (kk + 1) * width)], k == 0, k == KT - 1)
                if t == 1:
                    last.then_inc(units_used, 1)
                return last

            def sum_out(L, p, t, lhs_hi, lhs_lo, start, stop, j=0):
                split_ready(L, p, j)
                for kk in range(2):
                    last = products([acc[t][0][:, :], acc[t][1][:, :]], lhs_hi(kk), lhs_lo(kk), p % SLOTS,
                                    [slice(kk * D + n * 512, kk * D + (n + 1) * 512) for n in range(2)],
                                    start and kk == 0, stop and kk == 1)
                if t == 1:
                    last.then_inc(units_used, 1)
                return last

            def transpose_x(L, q, t):
                for half in range(2):
                    for i in range(4):
                        k = 4 * half + i
                        last = pe.transpose(TR[half][:, i * P:(i + 1) * P], xs[:, t, k * P:(k + 1) * P], ident[:, :])
                    last.then_inc(xT_psum, 1)

            def ffn(L, f):
                def enter(c, t, u, j=0):
                    if c == 0 and u == 0:
                        pe.wait_ge(xT_lo_done, n_tran(L, 2 * f, t, 1))
                    if c > 0 and u == 0:
                        pe.wait_ge(h_done, n_ffn(L, f, c - 1, t, j))
                    last = project(L, pos_in(f, c, u), t, u, U[t][:, :], 2 * FC, j)
                    if t == 0 and u == 1:
                        last.then_inc(gu_ready, 1)

                def transpose_h(c, t, j=0):
                    pe.wait_ge(h_done, n_ffn(L, f, c, t, j))
                    for kk in range(2):
                        last = pe.transpose(TR[t][:, kk * P:(kk + 1) * P], h[:, t, kk * P:(kk + 1) * P], ident[:, :])
                    last.then_inc(hT_psum, 1)

                def leave(c, t, j=0):
                    pe.wait_ge(hT_lo_done, n_ffn(L, f, c, t, j))
                    cols = slice(t * P, (t + 1) * P)
                    last = sum_out(L, pos_out(f, c), t, lambda kk: hT_hi[:, c % 2, kk, cols],
                                   lambda kk: hT_lo[:, c % 2, kk, cols], c == 0, c == NCH - 1, j)
                    if t == 0 and c == NCH - 1:
                        last.then_inc(acc_ready, 1)

                enter(0, 0, 0)
                if f == 1:
                    pe.wait_ge(x_new, n_x_new(L, 1, 1, 1))
                else:
                    pe.wait_ge(x_loaded[1], 16)
                    pe.wait_ge(x_new, n_x_new(L, -1, 1, 1))
                pe.wait_ge(xg_done, n_tran(L, 2 * f, 0, 1))
                transpose_x(L, 2 * f, 1)
                enter(0, 0, 1)
                enter(0, 1, 0)
                enter(0, 1, 1)

                def chunk(c, j=0):
                    enter(c, 0, 0, j)
                    enter(c, 0, 1, j)
                    transpose_h(c - 1, 0, j)
                    transpose_h(c - 1, 1, j)
                    enter(c, 1, 0, j)
                    enter(c, 1, 1, j)
                    leave(c - 1, 0, j)
                    leave(c - 1, 1, j)
                chunk(1)
                with pe.Fori(0, 3) as j:
                    chunk(2, j)
                    chunk(3, j)
                chunk(8)
                chunk(9)
                enter(10, 0, 0)
                enter(10, 0, 1)
                transpose_h(9, 0)
                transpose_h(9, 1)
                enter(10, 1, 0)
                enter(10, 1, 1)
                transpose_h(10, 0)
                leave(9, 0)
                leave(10, 0)
                transpose_h(10, 1)
                leave(9, 1)
                pe.wait_ge(x_new, n_x_new(L, 2 * f, 0, 1))
                pe.wait_ge(hT_lo_done, n_ffn(L, f, 10, 1))
                if f == 1:
                    with pe.If(L < DEPTH - 1):
                        transpose_x(L, 3, 0)
                else:
                    transpose_x(L, 1, 0)
                split_ready(L, pos_out(f, 10))
                for n in range(2):
                    for kk in range(2):
                        last = products([acc[1][n][:, :]], hT_hi[:, 0, kk, P:2 * P], hT_lo[:, 0, kk, P:2 * P],
                                        pos_out(f, 10) % SLOTS, [slice(kk * D + n * 512, kk * D + (n + 1) * 512)],
                                        False, kk == 1)
                    last.then_inc(half_sum if n == 0 else units_used, 1)

            def fill(L, name, blocks):
                n = FILLS.index(name)
                if n >= 2:
                    before = FILLS[n - 2]
                    if before in BY_DVE:
                        pe.wait_ge(tr_dve, n_of(L, BY_DVE, before))
                    else:
                        pe.wait_ge(tr_act, n_of(L, BY_ACT, before))
                else:
                    pe.wait_ge(xg_done, n_tran(L, 1, 1, n))
                for i, b in enumerate(blocks):
                    last = pe.transpose(TR[n % 2][:, i * P:(i + 1) * P], b, ident[:, :])
                last.then_inc(tr_filled, 1)

            def scores(L, r):
                t, half = divmod(r, 2)
                if r > 0:
                    pe.wait_ge(scores_biased, L * 4 + r)
                for i in range(4):
                    pair, rows_ = 2 * half + i // 2, slice((i % 2) * HD, (i % 2 + 1) * HD)
                    dst = acc[0][i % 2][:, (i // 2) * S:(i // 2 + 1) * S]
                    k_hi = kT_hi[rows_, half, :].rearrange("p (t n) -> p t n", t=2)
                    pe.matmul(dst, qT_hi[rows_, t, pair, :], k_hi, start=True, stop=False)
                    pe.matmul(dst, qT_hi[rows_, t, pair, :], kT_lo[rows_, :, half, :], start=False, stop=False)
                    last = pe.matmul(dst, qT_lo[rows_, t, pair, :], k_hi, start=False, stop=True)
                last.then_inc(scores_ready, 1)

            def probs_T(L, r):
                pe.wait_ge(probs_ready, L * 4 + (r + 1))
                for part in range(2):
                    fill(L, f"p{r}{'ab'[part]}", [sc[:, r % 2, 2 * part + i, b * P:(b + 1) * P]
                                                  for i in range(2) for b in range(2)])

            def weighted(L, r):
                t, half = divmod(r, 2)
                pe.wait_ge(tr_act, n_of(L, BY_ACT, f"p{r}a"))
                pe.wait_ge(tr_dve, n_of(L, BY_DVE, f"p{r}b"))
                for i in range(4):
                    hh = 4 * half + i
                    for b in range(2):
                        c = ((i % 2) * 2 + b) * P
                        last = pe.matmul(PV[:, hh * HD:(hh + 1) * HD], pT[:, i // 2, c:c + P],
                                         kv[:, b, (2 + half) * HD:(3 + half) * HD], start=(b == 0), stop=(b == 1))
                last.then_inc(pv_ready, 1)

            def spatial(L, t):
                pe.wait_ge(v_normed, L * 2 + (t + 1))
                for g in range(NG):
                    cols = slice(g * P, (g + 1) * P)
                    last = pe.matmul(SG[:, cols], wsT[:, cols], gv[:, t, cols], start=True, stop=True)
                last.then_inc(sg_ready, 1)

            def tiles(v, t):
                return [v[:, t, i * P:(i + 1) * P] for i in range(4)]

            def mix_out_of(L, i, t):
                cols = slice(t * P, (t + 1) * P)
                return sum_out(L, POS_OUT + i, t, lambda kk: xT_hi[:, OUT_TILES[i] + kk, cols],
                               lambda kk: xT_lo[:, OUT_TILES[i] + kk, cols], i == 0, i == 3)

            def warm_up(n):
                for _ in range(n):
                    pe.matmul(C1[:, 0:P], ident[:, :], ident[:, :], start=True, stop=True)

            pe.wait_ge(consts_ready, 1)
            warm_up(6)
            pe.wait_ge(gain_loaded, 16)
            pe.transpose(C0[:, 0:2 * KT], rows[0:2 * KT, :], ident[0:2 * KT, 0:2 * KT]).then_inc(rows_T, 1)
            pe.wait_ge(x_loaded[0], 16)
            transpose_x(0, 0, 0)
            warm_up(6)
            pe.wait_ge(rows_loaded, 16 * 2)
            pe.wait_ge(head_rows_loaded, 16 * 3)
            pe.wait_ge(gain_taken, 1)
            pe.transpose(C0[:, 0:NROW], rows, ident[0:NROW, 0:NROW]).then_inc(rows_T, 1)
            warm_up(4)
            with pe.Fori(0, DEPTH) as L:
                ffn(L, 0)
                pe.wait_ge(xT_lo_done, n_tran(L, 1, 0, 1))
                project(L, POS_KV, 0, 0, U[0][:, 0:4 * HD], 4 * HD).then_inc(proj_ready, 1)
                pe.wait_ge(x_new, n_x_new(L, 0, 1, 1))
                pe.wait_ge(xg_done, n_tran(L, 1, 0, 1))
                transpose_x(L, 1, 1)
                project(L, POS_Q, 0, 0, C0[:, :], MIX_A)
                pe.wait_ge(mix_params, L * 48 + 48)
                fill(L, "ws", [ws[:, g, :] for g in range(NG)])
                project(L, POS_Q + 1, 0, 1, C0[:, :], MIX_A).then_inc(proj_ready, 1)
                pe.wait_ge(xT_lo_done, n_tran(L, 1, 1, 1))
                project(L, POS_KV, 1, 0, U[1][:, 0:4 * HD], 4 * HD)
                pe.wait_ge(k_normed, L * 2 + 1)
                fill(L, "k0", [kd[:, 0, g, :] for g in range(2)])
                project(L, POS_Q, 1, 0, C1[:, :], MIX_A)
                project(L, POS_Q + 1, 1, 1, C1[:, :], MIX_A)
                pe.wait_ge(q_normed, L * 2 + 1)
                fill(L, "q0", tiles(qs, 0))
                pe.wait_ge(proj_taken, n_of(L, TAKEN, "KV0"))
                project(L, POS_V, 0, 0, U[0][:, :], MIX_A)
                pe.wait_ge(k_normed, L * 2 + 2)
                fill(L, "k1", [kd[:, 1, g, :] for g in range(2)])
                project(L, POS_V + 1, 0, 1, U[0][:, :], MIX_A).then_inc(proj_ready, 1)
                pe.wait_ge(tr_dve, n_of(L, BY_DVE, "k1"))
                pe.wait_ge(proj_taken, n_of(L, TAKEN, "Q1"))
                scores(L, 0)
                pe.wait_ge(q_normed, L * 2 + 2)
                fill(L, "q1", tiles(qs, 1))
                project(L, POS_V, 1, 0, U[1][:, :], MIX_A)
                project(L, POS_V + 1, 1, 1, U[1][:, :], MIX_A)
                pe.wait_ge(tr_dve, n_of(L, BY_DVE, "q1"))
                scores(L, 1)
                probs_T(L, 0)
                project(L, POS_U, 0, 0, acc[1][0][:, :], MIX_A)
                scores(L, 2)
                weighted(L, 0)
                probs_T(L, 1)
                scores(L, 3)
                project(L, POS_U + 1, 0, 1, acc[1][0][:, :], MIX_A).then_inc(proj_ready, 1)
                weighted(L, 1)
                pe.wait_ge(proj_taken, n_of(L, TAKEN, "V1"))
                spatial(L, 0)
                probs_T(L, 2)
                project(L, POS_U, 1, 0, U[0][:, :], MIX_A)
                pe.wait_ge(o_done, L * 2 + 1)
                fill(L, "o0", [o[:, i * P:(i + 1) * P] for i in range(4)])
                weighted(L, 2)
                probs_T(L, 3)
                project(L, POS_U + 1, 1, 1, U[0][:, :], MIX_A)
                pe.wait_ge(a_done, L * 2 + 1)
                spatial(L, 1)
                weighted(L, 3)
                fill(L, "a0", tiles(qs, 0))
                pe.wait_ge(scores_biased, L * 4 + 4)
                pe.wait_ge(tr_dve, n_of(L, BY_DVE, "o0"))
                mix_out_of(L, 0, 0)
                pe.wait_ge(o_done, L * 2 + 2)
                fill(L, "o1", [o[:, i * P:(i + 1) * P] for i in range(4)])
                mix_out_of(L, 1, 0)
                pe.wait_ge(a_done, L * 2 + 2)
                fill(L, "a1", tiles(qs, 1))
                pe.wait_ge(tr_dve, n_of(L, BY_DVE, "a0"))
                mix_out_of(L, 2, 0)
                mix_out_of(L, 3, 0).then_inc(acc_ready, 1)
                pe.wait_ge(tr_dve, n_of(L, BY_DVE, "o1"))
                mix_out_of(L, 0, 1)
                mix_out_of(L, 1, 1)
                pe.wait_ge(tr_dve, n_of(L, BY_DVE, "a1"))
                mix_out_of(L, 2, 1)
                pe.wait_ge(x_new, n_x_new(L, 1, 0, 1))
                transpose_x(L, 2, 0)
                mix_out_of(L, 3, 1)
                ffn(L, 1)


_INS = ["x", "ffn1_norm", "ffn1_w_in", "ffn1_w_out", "mix_norm", "w_mix_in", "sgu_norm", "sgu_w", "sgu_b",
        "q_norm", "k_norm", "sink", "rel_bias", "w_mix_out", "ffn2_norm", "ffn2_w_in", "ffn2_w_out"]


def kernel(**inputs):
    import numpy as _np
    import concourse.bacc as _bacc
    from concourse import mybir as _mybir
    from concourse.bass_utils import run_bass_kernel_spmd as _run

    nc = _bacc.Bacc("TRN2", target_bir_lowering=False, num_devices=1)
    arrays, args = {}, []
    for name in _INS:
        a = _np.ascontiguousarray(inputs[name])
        arrays[f"in_{name}_dram"] = a
        args.append(nc.dram_tensor(f"in_{name}_dram", a.shape, _mybir.dt.from_np(a.dtype), kind="ExternalInput").ap())
    args.append(nc.dram_tensor("out_0_dram", arrays["in_x_dram"].shape, _mybir.dt.float32, kind="ExternalOutput").ap())
    encoder(nc, *args)
    r = _run(nc, [arrays], core_ids=[0])
    return r.results[0]["out_0_dram"]
```
